# Optimizing a Trainium2 kernel written in Bass

```python
import jax, jax.numpy as jnp
from jax import lax
import numpy as np

D_MODEL = 1024
BATCH = 1
SEQ = 128
DEPTH = 2
DEC_BATCH = 1
DEC_SEQ = 512
PAST_LEN = 128

GRID_W = 64
HEAD_DIM = 64
A_HEADS = 4
A_WIDTH = A_HEADS * HEAD_DIM
A_CHUNK = 16
B_Q_HEADS = 6
B_KV_HEADS = 2
B_Q_WIDTH = B_Q_HEADS * HEAD_DIM
B_KV_WIDTH = B_KV_HEADS * HEAD_DIM
C_Q_HEADS = 6
C_KV_HEADS = 2
C_Q_WIDTH = C_Q_HEADS * HEAD_DIM
C_KV_WIDTH = C_KV_HEADS * HEAD_DIM
WINDOW = 128
Q_BLOCK = 128
ROPE_THETA = 10000.0
MIX_WIDTH = A_WIDTH + B_Q_WIDTH + C_Q_WIDTH
IN_WIDTH = 5 * A_WIDTH + B_Q_WIDTH + 2 * B_KV_WIDTH + C_Q_WIDTH + 2 * C_KV_WIDTH
N_EXPERTS = 16
N_GROUPS = 4
EXPERTS_PER_GROUP = N_EXPERTS // N_GROUPS
TOP_K = 2
D_EXPERT = 256
EPS = 1e-6
MASK_VALUE = -1e30
TINY = 1e-30

kernel_name = 'hybrid_diffusion_prefix_step'

def rms_norm(x, g):
    xf = x.astype(jnp.float32)
    y = xf * lax.rsqrt(jnp.mean(xf * xf, axis=-1, keepdims=True) + EPS)
    return (y * g.astype(jnp.float32)).astype(x.dtype)

def to_heads(a):
    return a.reshape(*a.shape[:-1], a.shape[-1] // HEAD_DIM, HEAD_DIM)

def split_proj(z):
    sizes = (A_WIDTH,) * 5 + (B_Q_WIDTH, B_KV_WIDTH, B_KV_WIDTH, C_Q_WIDTH, C_KV_WIDTH, C_KV_WIDTH)
    cuts = [int(v) for v in np.cumsum(sizes)[:-1]]
    return jnp.split(z, cuts, axis=-1)

def rope_2d(x):
    T = x.shape[1]
    rows = T // GRID_W
    row = jnp.broadcast_to(jnp.arange(rows)[:, None], (rows, GRID_W)).reshape(-1)
    col = jnp.broadcast_to(jnp.arange(GRID_W)[None, :], (rows, GRID_W)).reshape(-1)
    pos = jnp.stack([row, col], 0).astype(jnp.float32)
    n_freq = HEAD_DIM // 4
    freqs = ROPE_THETA ** (-jnp.arange(n_freq, dtype=jnp.float32) / n_freq)
    ang = jnp.transpose(pos[:, :, None] * freqs, (1, 0, 2))[None, :, None]
    cos, sin = jnp.cos(ang), jnp.sin(ang)
    xf = x.astype(jnp.float32).reshape(*x.shape[:-1], 2, 2, n_freq)
    x1, x2 = xf[..., 0, :], xf[..., 1, :]
    out = jnp.stack([x1 * cos - x2 * sin, x1 * sin + x2 * cos], axis=-2)
    return out.reshape(x.shape).astype(x.dtype)

def blocked_attention(q, k, v, sink=None):
    B, Tq, Hq, D = q.shape
    Hkv = k.shape[2]
    G = Hq // Hkv
    nb = Tq // Q_BLOCK
    qb = q.reshape(B, nb, Q_BLOCK, Hkv, G, D).transpose(1, 0, 2, 3, 4, 5)
    scale = D ** -0.5

    def one_block(qi):
        s = jnp.einsum('bqkgd,bskd->bkgqs', qi, k).astype(jnp.float32) * scale
        if sink is not None:
            sk = jnp.broadcast_to(sink.astype(jnp.float32).reshape(Hkv, G, 1, 1), s.shape[:-1] + (1,))
            p = jax.nn.softmax(jnp.concatenate([s, sk], axis=-1), axis=-1)[..., :-1]
        else:
            p = jax.nn.softmax(s, axis=-1)
        return jnp.einsum('bkgqs,bskd->bqkgd', p.astype(v.dtype), v)

    o = lax.map(one_block, qb)
    return o.transpose(1, 0, 2, 3, 4, 5).reshape(B, Tq, Hq * D)

def banded_attention(q, k, v, k_ctx, v_ctx, sink):
    B, T, Hq, D = q.shape
    Hkv = k.shape[2]
    G = Hq // Hkv
    L = k_ctx.shape[1]
    nb = T // Q_BLOCK
    scale = D ** -0.5

    def neighbours(a):
        ap = jnp.pad(a, ((0, 0), (Q_BLOCK, Q_BLOCK), (0, 0), (0, 0))).reshape(B, nb + 2, Q_BLOCK, Hkv, D)
        return jnp.concatenate([ap[:, :-2], ap[:, 1:-1], ap[:, 2:]], axis=2)

    kb, vb = neighbours(k), neighbours(v)
    qb = q.reshape(B, nb, Q_BLOCK, Hkv, G, D)
    s_loc = jnp.einsum('bnqkgd,bnskd->bnkgqs', qb, kb).astype(jnp.float32) * scale
    qpos = jnp.arange(nb)[:, None] * Q_BLOCK + jnp.arange(Q_BLOCK)[None, :]
    kpos = (jnp.arange(nb)[:, None] - 1) * Q_BLOCK + jnp.arange(3 * Q_BLOCK)[None, :]
    valid = ((kpos[:, None, :] >= 0) & (kpos[:, None, :] < T)
             & (jnp.abs(qpos[:, :, None] - kpos[:, None, :]) <= WINDOW))
    s_loc = jnp.where(valid[None, :, None, None], s_loc, MASK_VALUE)
    s_ctx = jnp.einsum('bnqkgd,bskd->bnkgqs', qb, k_ctx).astype(jnp.float32) * scale
    sk = jnp.broadcast_to(sink.astype(jnp.float32).reshape(1, 1, Hkv, G, 1, 1), s_loc.shape[:-1] + (1,))
    p = jax.nn.softmax(jnp.concatenate([s_loc, s_ctx, sk], axis=-1), axis=-1).astype(v.dtype)
    o = (jnp.einsum('bnkgqs,bnskd->bnqkgd', p[..., :3 * Q_BLOCK], vb)
         + jnp.einsum('bnkgqs,bskd->bnqkgd', p[..., 3 * Q_BLOCK:3 * Q_BLOCK + L], v_ctx))
    return o.reshape(B, T, Hq * D)

def hgrn_lower_bounds(lb_logits):
    p = jax.nn.softmax(lb_logits.astype(jnp.float32), axis=1)
    return jnp.cumsum(p, axis=1) - p[:, :1]

def hgrn_scan(q, k, v, log_f, s0):
    B, T, H, K = q.shape
    n = T // A_CHUNK

    def chunks(a):
        return a.reshape(B, n, A_CHUNK, H, a.shape[-1]).transpose(1, 0, 3, 2, 4)

    qc, kc, vc, gc = chunks(q), chunks(k), chunks(v), chunks(log_f)
    b = jnp.cumsum(gc, axis=3)
    causal = jnp.tril(jnp.ones((A_CHUNK, A_CHUNK), dtype=bool))[:, :, None]
    diff = b[..., :, None, :] - b[..., None, :, :]
    decay = jnp.where(causal, jnp.exp(jnp.where(causal, diff, 0.0)), 0.0)
    scores = jnp.einsum('nbhtk,nbhsk,nbhtsk->nbhts', qc, kc, decay)
    o_intra = jnp.einsum('nbhts,nbhsv->nbhtv', scores, vc)
    q_in = qc * jnp.exp(b)
    k_out = kc * jnp.exp(b[..., -1:, :] - b)
    d_chunk = jnp.exp(b[..., -1, :])

    def step(S, xs):
        qi, ki, vi, di = xs
        o = jnp.einsum('bhtk,bhkv->bhtv', qi, S)
        S = di[..., None] * S + jnp.einsum('bhsk,bhsv->bhkv', ki, vi)
        return S, o

    s_fin, o_inter = lax.scan(step, s0, (q_in, k_out, vc, d_chunk))
    o = (o_intra + o_inter).transpose(1, 0, 3, 2, 4).reshape(B, T, H, v.shape[-1])
    return o, s_fin

def hgrn_mixer(qa, ia, fza, fzb, ga, lb, norm_g, s0):
    f32 = jnp.float32
    hd = lambda a: to_heads(a.astype(f32))
    q = jax.nn.silu(hd(qa))
    v = hd(ia)

    def gates(z, lb_d):
        lb_d = lb_d.reshape(A_HEADS, HEAD_DIM)
        f = lb_d + (1.0 - lb_d) * jax.nn.sigmoid(z)
        log_f = jnp.log(jnp.maximum(f, TINY))
        k = (1.0 - lb_d) * jax.nn.sigmoid(-z)
        return log_f, k

    lf_f, k_f = gates(hd(fza), lb[0])
    lf_b, k_b = gates(hd(fzb), lb[1])
    rev = lambda a: a[:, ::-1]
    o_f, s_f = hgrn_scan(q, k_f, v, lf_f, s0[:, 0])
    o_b, s_b = hgrn_scan(rev(q), rev(k_b), rev(v), rev(lf_b), s0[:, 1])
    o = rms_norm(o_f + rev(o_b), norm_g) * jax.nn.sigmoid(hd(ga))
    return o.reshape(*qa.shape[:-1], A_WIDTH).astype(qa.dtype), jnp.stack([s_f, s_b], axis=1)

def moe(h, router_w, router_b, w_gate_up, w_down):
    B, T, D = h.shape
    hf = h.reshape(B * T, D)
    scores = jax.nn.sigmoid((hf @ router_w).astype(jnp.float32))
    sel = scores + router_b.astype(jnp.float32)
    group_score = lax.top_k(sel.reshape(-1, N_GROUPS, EXPERTS_PER_GROUP), 2)[0].sum(-1)
    gid = jnp.argmax(group_score, axis=-1)
    in_group = (jnp.arange(N_EXPERTS) // EXPERTS_PER_GROUP)[None, :] == gid[:, None]
    _, idx = lax.top_k(jnp.where(in_group, sel, MASK_VALUE), TOP_K)
    w = jnp.take_along_axis(scores, idx, axis=-1)
    w = w / jnp.sum(w, axis=-1, keepdims=True)
    combine = jnp.sum(jax.nn.one_hot(idx, N_EXPERTS, dtype=jnp.float32) * w[..., None], axis=1)
    gu = jnp.einsum('nd,edf->nef', hf, w_gate_up)
    g, u = jnp.split(gu, 2, axis=-1)
    act = jax.nn.silu(g) * u * combine[..., None].astype(h.dtype)
    return jnp.einsum('nef,efd->nd', act, w_down).reshape(B, T, D)

def trunk_layer(x, cond, lb, cached, mod_w, mod_b, norm1_g, norm2_g, w_in, w_out, a_norm_g,
                q_norm_g, k_norm_g, sink, router_w, router_b, w_gate_up, w_down):
    mod = jax.nn.silu(cond) @ mod_w + mod_b
    sh1, sc1, g1, sh2, sc2, g2 = jnp.split(mod[:, None, :], 6, axis=-1)
    h = rms_norm(x, norm1_g) * (1.0 + sc1) + sh1
    qa, ia, fza, fzb, ga, qg, kg, vg, qw, kw, vw = split_proj(h @ w_in)
    qg = rms_norm(to_heads(qg), q_norm_g)
    kg = rms_norm(to_heads(kg), k_norm_g)
    vg, qw, kw, vw = to_heads(vg), to_heads(qw), to_heads(kw), to_heads(vw)
    if cached is None:
        s0 = jnp.zeros((x.shape[0], 2, A_HEADS, HEAD_DIM, HEAD_DIM), jnp.float32)
        o_a, s_a = hgrn_mixer(qa, ia, fza, fzb, ga, lb, a_norm_g, s0)
        o_g = blocked_attention(qg, kg, vg)
        o_w = blocked_attention(qw, kw, vw, sink)
        new = (kg, vg, kw, vw, s_a.astype(x.dtype))
    else:
        ck_g, cv_g, ck_w, cv_w, s_ctx = cached
        o_a, _ = hgrn_mixer(qa, ia, fza, fzb, ga, lb, a_norm_g, s_ctx.astype(jnp.float32))
        o_g = blocked_attention(rope_2d(qg), jnp.concatenate([rope_2d(kg), ck_g], axis=1),
                                jnp.concatenate([vg, cv_g], axis=1))
        o_w = banded_attention(rope_2d(qw), rope_2d(kw), vw, ck_w, cv_w, sink)
        new = None
    x = x + g1 * (jnp.concatenate([o_a, o_g, o_w], axis=-1) @ w_out)
    h = rms_norm(x, norm2_g) * (1.0 + sc2) + sh2
    x = x + g2 * moe(h, router_w, router_b, w_gate_up, w_down)
    return x, new

def setup_inputs(seed: int = 0) -> dict:
    key = jax.random.key(seed)
    ks = jax.random.split(key, 25)
    nrm = lambda k, shape, s=1.0: jax.random.normal(k, shape, jnp.float32) * s
    return {
        'x_prompt': nrm(ks[0], (BATCH, SEQ, D_MODEL)),
        'x_sample': nrm(ks[1], (DEC_BATCH, DEC_SEQ, D_MODEL)),
        'cache_glob_k': nrm(ks[2], (DEC_BATCH, DEPTH, PAST_LEN, B_KV_HEADS, HEAD_DIM)),
        'cache_glob_v': nrm(ks[3], (DEC_BATCH, DEPTH, PAST_LEN, B_KV_HEADS, HEAD_DIM)),
        'cache_win_k': nrm(ks[4], (DEC_BATCH, DEPTH, PAST_LEN, C_KV_HEADS, HEAD_DIM)),
        'cache_win_v': nrm(ks[5], (DEC_BATCH, DEPTH, PAST_LEN, C_KV_HEADS, HEAD_DIM)),
        'state_hgrn': nrm(ks[6], (DEC_BATCH, DEPTH, 2, A_HEADS, HEAD_DIM, HEAD_DIM), 0.5),
        'c': nrm(ks[7], (DEC_BATCH, D_MODEL)),
        'c_ctx': nrm(ks[8], (D_MODEL,)),
        'mod_w': nrm(ks[9], (DEPTH, D_MODEL, 6 * D_MODEL), 0.5 * D_MODEL ** -0.5),
        'mod_b': nrm(ks[10], (DEPTH, 6 * D_MODEL), 0.02),
        'norm1_g': 1.0 + nrm(ks[11], (DEPTH, D_MODEL), 0.02),
        'norm2_g': 1.0 + nrm(ks[12], (DEPTH, D_MODEL), 0.02),
        'w_in': nrm(ks[13], (DEPTH, D_MODEL, IN_WIDTH), D_MODEL ** -0.5),
        'w_out': nrm(ks[14], (DEPTH, MIX_WIDTH, D_MODEL), MIX_WIDTH ** -0.5),
        'hgrn_lb': nrm(ks[15], (2, DEPTH, A_WIDTH)),
        'hgrn_norm_g': 1.0 + nrm(ks[16], (DEPTH, HEAD_DIM), 0.02),
        'q_norm_g': 1.0 + nrm(ks[17], (DEPTH, HEAD_DIM), 0.02),
        'k_norm_g': 1.0 + nrm(ks[18], (DEPTH, HEAD_DIM), 0.02),
        'win_sink': nrm(ks[19], (DEPTH, C_Q_HEADS), 0.5),
        'router_w': nrm(ks[20], (D_MODEL, N_EXPERTS), D_MODEL ** -0.5),
        'router_b': nrm(ks[21], (N_EXPERTS,), 0.01),
        'w_gate_up': nrm(ks[22], (DEPTH, N_EXPERTS, D_MODEL, 2 * D_EXPERT), D_MODEL ** -0.5),
        'w_down': nrm(ks[23], (DEPTH, N_EXPERTS, D_EXPERT, D_MODEL), D_EXPERT ** -0.5),
        'final_g': 1.0 + nrm(ks[24], (D_MODEL,), 0.02),
    }

def reference(x_prompt, x_sample, cache_glob_k, cache_glob_v, cache_win_k, cache_win_v, state_hgrn,
              c, c_ctx, mod_w, mod_b, norm1_g, norm2_g, w_in, w_out, hgrn_lb, hgrn_norm_g,
              q_norm_g, k_norm_g, win_sink, router_w, router_b, w_gate_up, w_down, final_g):
    lbs = hgrn_lower_bounds(hgrn_lb)
    xp, xs = x_prompt, x_sample
    gk, gv, wk, wv, sa = [], [], [], [], []
    for l in range(DEPTH):
        params = (mod_w[l], mod_b[l], norm1_g[l], norm2_g[l], w_in[l], w_out[l], hgrn_norm_g[l],
                  q_norm_g[l], k_norm_g[l], win_sink[l], router_w, router_b, w_gate_up[l], w_down[l])
        xp, ctx_out = trunk_layer(xp, c_ctx[None, :], lbs[:, l], None, *params)
        gk.append(ctx_out[0]); gv.append(ctx_out[1]); wk.append(ctx_out[2]); wv.append(ctx_out[3]); sa.append(ctx_out[4])
        cached = (cache_glob_k[:, l], cache_glob_v[:, l], cache_win_k[:, l], cache_win_v[:, l], state_hgrn[:, l])
        xs, _ = trunk_layer(xs, c, lbs[:, l], cached, *params)
    y_prompt = rms_norm(xp, final_g)
    y_sample = rms_norm(xs, final_g)
    new_glob_k = jnp.stack(gk, axis=1)
    new_glob_v = jnp.stack(gv, axis=1)
    new_win_k = jnp.stack(wk, axis=1)
    new_win_v = jnp.stack(wv, axis=1)
    new_state_hgrn = jnp.stack(sa, axis=1)
    return (y_prompt, y_sample, new_glob_k, new_glob_v, new_win_k, new_win_v, new_state_hgrn)


_drawn_inputs = setup_inputs


def setup_inputs(seed=0):
    import zlib

    import numpy as np

    out = dict(_drawn_inputs(seed))
    spreads = {}
    factors = {'cache_glob_v': 2.785,
     'state_hgrn': 32.965,
     'norm1_g': 2.912,
     'hgrn_norm_g': 4.514,
     'q_norm_g': 8.0,
     'k_norm_g': 2.977,
     'win_sink': 64.0,
     'final_g': 22.123,
     'cache_glob_k': 8.0,
     'cache_win_k': 8.0,
     'cache_win_v': 8.0}
    for name, (base, spread) in spreads.items():
        noise = np.random.default_rng([zlib.crc32(name.encode()), seed]).standard_normal(out[name].shape)
        drawn = base * np.exp(spread * noise) if base else spread * noise
        out[name] = __import__('jax').numpy.asarray(drawn.astype(out[name].dtype))
    for name, factor in factors.items():
        out[name] = (out[name] * factor).astype(out[name].dtype)
    return out
```

```python
from contextlib import ExitStack

import concourse.bass as bass
from concourse import mybir

F32 = mybir.dt.float32
I32 = mybir.dt.int32
U8 = mybir.dt.uint8
ALU = mybir.AluOpType
ACT = mybir.ActivationFunctionType
AX = mybir.AxisListType

P = 128
D = 1024
KC = D // P
DEPTH = 2
NL = 4
NT = NL + 1
TOK = NT * P
HD = 64
AH = 4
AW = AH * HD
QH = 6
KVH = 2
G = QH // KVH
QW = QH * HD
KVW = KVH * HD
INW = 5 * AW + 2 * (QW + 2 * KVW)
NE = 16
EPG = 4
NG = NE // EPG
DE = 256
EPS = 1e-6
TINY = 1e-30
SCALE = HD ** -0.5
LEVELS = [1, 2, 4, 8, 16, 32, 64]
KEYS = TOK + P
MODC = 6 * KC
C_IDENT, C_WIN, C_COS, C_SIN, C_LT = 0, 128, 640, 896, 1152
C_END = C_LT + 16


T_SIZE = 19456
NS = (2 * TOK + NE * (P - 1)) // P
RC_BEFORE, RC_ONES, RC_TILE, RC_TOKEN = 0, P, 2 * P, 2 * P + NS
RC_END = RC_TOKEN + NT


def col(t, n=P):
    return slice(t * n, (t + 1) * n)


def program(nc, x_prompt, x_sample, cgk, cgv, cwk, cwv, state, c, c_ctx, mod_w, mod_b, norm1_g, norm2_g,
            w_in, w_out, hgrn_lb, hgrn_norm_g, q_norm_g, k_norm_g, win_sink, router_w, router_b,
            w_gate_up, w_down, final_g, consts, masks, route_consts,
            y_prompt, y_sample, new_gk, new_gv, new_wk, new_wv, new_state):
    ctx = ExitStack()
    with ctx:
        def sb(name, shape, dt=F32):
            return ctx.enter_context(nc.sbuf_tensor(name, shape, dt))

        def sem(name):
            return ctx.enter_context(nc.semaphore(name))

        cst = sb("cst", [P, C_END])
        ident = cst[:, C_IDENT:C_IDENT + P]
        winmask = cst[:, C_WIN:C_WIN + 512]
        cosT = cst[:, C_COS:C_COS + 2 * P].rearrange("p (t m f) -> p t m f", t=NL, m=4)
        sinT = cst[:, C_SIN:C_SIN + 2 * P].rearrange("p (t m f) -> p t m f", t=NL, m=4)
        ltmask = cst[:, C_LT:C_LT + 16]
        levelmask = sb("levelmask", [P, 2, len(LEVELS) + 1, P], U8)
        x = sb("x", [P, NT, D])
        hT = sb("hT", [P, KC, TOK])
        W = sb("W", [P, KC * INW])
        condT = sb("condT", [P, KC, 2])
        lball = sb("lball", [P, DEPTH, 2, 2])
        lb = sb("lb", [P, 2, 2])
        olb = sb("olb", [P, 2, 2])
        modc = sb("modc", [P, MODC, 2])
        scale1 = sb("scale1", [P, KC, 2])
        scale2 = sb("scale2", [P, KC, 2])
        small = sb("small", [P, 512])
        minus_half = sb("minus_half", [P, 64])
        qkg = sb("qkg", [P, 2, HD])
        ang = sb("ang", [P, HD])
        sink = sb("sink", [P, QH])
        rbias = sb("rbias", [P, NE])
        T = sb("T", [P, T_SIZE])
        PS = ctx.enter_context(nc.psum_tensor("PS", [P, 8, 512], F32))

        top = [0]

        def carve(n, **shape):
            a = T[:, top[0]:top[0] + n]
            top[0] += n
            return a

        va = carve(NT * AW).rearrange("p (t n) -> p t n", t=NT)
        ga = carve(NT * AW).rearrange("p (t n) -> p t n", t=NT)
        vg = carve((NT + 1) * KVW).rearrange("p (t n) -> p t n", t=NT + 1)
        vw = carve((NT + 1) * KVW).rearrange("p (t n) -> p t n", t=NT + 1)
        qT = carve(2 * G * TOK).rearrange("p (w j n) -> p w j n", w=2, j=G)
        kT = carve(2 * KEYS).rearrange("p (w n) -> p w n", w=2)
        QQ = carve(2 * TOK).rearrange("p (f n) -> p f n", f=2)
        QF = carve(4 * TOK).rearrange("p (d f n) -> p d f n", d=2, f=2)
        KK = carve(4 * TOK).rearrange("p (d f n) -> p d f n", d=2, f=2)
        tail = top[0]
        zs = carve(2 * 1792).rearrange("p (s n) -> p s n", s=2)
        xn = zs.rearrange("p s n -> p (s n)")[:, 0:2 * D].rearrange("p (s n) -> p s n", s=2)
        assert top[0] <= T_SIZE, top[0]
        modw = T[:, 0:2 * KC * 512].rearrange("p (s k n) -> p s k n", s=2, k=KC)
        modrow = T[:, 2 * KC * 512 + 3 * P:2 * KC * 512 + 3 * P + 1024].rearrange("p (s n) -> p s n", s=2)
        rows = T[:, 2 * KC * 512:2 * KC * 512 + 3 * P].rearrange("p (s n) -> p s n", s=3)
        win = W[:, :].rearrange("p (k n) -> p k n", k=KC)
        wout = W[:, 0:KC * D].rearrange("p (k n) -> p k n", k=KC)
        exps = W[:, KC * D:KC * D + 2 * 6144].rearrange("p (s n) -> p s n", s=2)
        M = W[:, KC * D:KC * D + 4 * TOK].rearrange("p (d f n) -> p d f n", d=2, f=2)
        KF = W[:, KC * D + 4 * TOK:KC * D + 8 * TOK].rearrange("p (d f n) -> p d f n", d=2, f=2)
        Am = hT[:, :, :].rearrange("p k n -> p (k n)").rearrange("p (d t a n) -> p d t a n", d=2, t=NT, a=AH)
        sv0 = KC * D + 8 * TOK
        Sv = W[:, sv0:sv0 + 2048].rearrange("p (d s f n) -> p d s f n", d=2, s=4, f=2)
        modw2 = W[:, 0:2 * KC * 512].rearrange("p (s k n) -> p s k n", s=2, k=KC)
        modrow2 = T[:, tail + 2560:tail + 3584].rearrange("p (s n) -> p s n", s=2)
        oall = W[:, KC * INW - NT * D:].rearrange("p (t n) -> p t n", t=NT)
        assert sv0 + 2048 <= KC * INW - NT * D
        kout = T[:, tail:tail + 2 * AW].rearrange("p (s n) -> p s n", s=2)
        Sc = T[:, tail + 1024:tail + 1024 + 256].rearrange("p (d f n) -> p d f n", d=2, f=2)
        osq = T[:, tail + 1280:tail + 1280 + NT * AW].rearrange("p (t n) -> p t n", t=NT)
        at0 = tail
        pr = T[:, at0:at0 + 2 * 640].rearrange("p (s n) -> p s n", s=2)
        prT = T[:, at0 + 1280:at0 + 2560].rearrange("p (s n) -> p s n", s=2)
        sm = T[:, at0 + 2560:at0 + 3584].rearrange("p (s n) -> p s n", s=2)
        g1b = T[:, tail:tail + 2 * D].rearrange("p (s n) -> p s n", s=2)
        oT = T[:, 0:2 * KC * P].rearrange("p (s k n) -> p s k n", s=2, k=KC)
        prod = T[:, 2048:2048 + 2 * D].rearrange("p (s n) -> p s n", s=2)
        tt = [0]

        def carve2(n):
            a = T[:, tt[0]:tt[0] + n]
            tt[0] += n
            return a

        g2b = carve2(2 * D).rearrange("p (s n) -> p s n", s=2)
        rw = carve2(KC * NE).rearrange("p (k n) -> p k n", k=KC)
        rc = carve2(RC_END)
        slot_f = carve2(2 * NT).rearrange("p (c t) -> p c t", c=2)
        wpair = carve2(2 * NT).rearrange("p (c t) -> p c t", c=2)
        slot_i = carve2(2 * NT).bitcast(I32).rearrange("p (c t) -> p c t", c=2)
        token_i = carve2(NT).bitcast(I32)
        slot_token = carve2(NS).bitcast(I32)
        tile_expert = carve2(NS).bitcast(I32)
        zero_i = carve2(NS).bitcast(I32)
        e0 = tt[0]
        arow = carve2(2 * D).rearrange("p (s n) -> p s n", s=2)
        brow = carve2(2 * D).rearrange("p (s n) -> p s n", s=2)
        h2 = carve2(NT * D).rearrange("p (t n) -> p t n", t=NT)
        rt = carve2(4096)
        assert tt[0] <= T_SIZE
        tt[0] = e0
        hg = carve2(2 * D).rearrange("p (s n) -> p s n", s=2)
        hgT = carve2(2 * D).rearrange("p (s k n) -> p s k n", s=2, k=KC)
        ys = carve2(2 * D).rearrange("p (s n) -> p s n", s=2)
        sg, ha, haT = (carve2(2 * DE).rearrange("p (s n) -> p s n", s=2) for _ in range(3))
        yab = carve2(4 * D).rearrange("p (s c n) -> p s c n", s=2, c=2)
        assert tt[0] <= T_SIZE
        h_dram = nc.dram_tensor("h_rows", (TOK, D), F32, kind="Internal").ap()
        y_dram = nc.dram_tensor("y_rows", (NS * P, D), F32, kind="Internal").ap()
        slot_dram = nc.dram_tensor("slot_tokens", (NS * P, 1), I32, kind="Internal").ap()

        def chain(eng, s, start=0):
            count = [start]

            def link(ins):
                count[0] += 1
                ins.then_inc(s, 1)
                eng.wait_ge(s, count[0])
            return link

        with ExitStack() as st:
            def ssem(name):
                return st.enter_context(nc.semaphore(name))
            s_ld, s_pe, s_v, s_a, s_g = (ssem(n) for n in ("set_load", "set_pe", "set_vec", "set_act", "set_pool"))
            crow = T[0:8, 0:3 * P].rearrange("p (s n) -> p s n", s=3)
            mask_f32 = T[:, 1024:1024 + 2 * (len(LEVELS) + 1) * P]
            lbc = small[:, 0:8].rearrange("p (d l f) -> p d l f", d=2, l=DEPTH)
            block = st.enter_context(nc.Block())

            @block.sync
            def _(sp):
                sp.dma_start(cst[:, :], consts).then_inc(s_ld, 16)
                sp.dma_start(mask_f32, masks).then_inc(s_ld, 16)
                sp.dma_start(crow[:, 0, :], c_ctx.rearrange("(a b) -> a b", b=P)).then_inc(s_ld, 16)
                sp.dma_start(crow[:, 1, :], c.rearrange("o (a b) -> (o a) b", b=P)).then_inc(s_ld, 16)
                sp.dma_start(crow[:, 2, :], hgrn_lb.rearrange("d l (f b) -> (d l f) b", b=P)).then_inc(s_ld, 16)
                sp.dma_start(x[:, 0, :], x_prompt[0]).then_inc(s_ld, 16)
                sp.dma_start(x[:, 1:NT, :], x_sample[0].rearrange("(t p) n -> p t n", p=P)).then_inc(s_ld, 16)
                sp.dma_start(rbias[:, :], router_b.partition_broadcast(P)).then_inc(s_ld, 16)
                sp.wait_ge(s_ld, 8 * 16)

            @block.gpsimd
            def _(pool):
                pool.memset(minus_half[:, :], -0.5).then_inc(s_g, 1)
                pool.wait_ge(s_g, 1)

            @block.tensor
            def _(pe):
                pe.wait_ge(s_ld, 8 * 16)
                for s in range(3):
                    last = pe.transpose(PS[:, 0, s * 8:s * 8 + 8], crow[:, s, :], ident[0:8, 0:8])
                last.then_inc(s_pe, 1)

            @block.scalar
            def _(act):
                act.wait_ge(s_v, 1)
                act.activation(small[:, 16:32], PS[:, 0, 0:16], ACT.Sigmoid).then_inc(s_a, 1)
                act.wait_ge(s_v, 3)
                act.activation(small[:, 48:56], small[:, 40:48], ACT.Exp).then_inc(s_a, 1)

            @block.vector
            def _(dve):
                link = chain(dve, s_v)
                dve.wait_ge(s_pe, 1)
                link(dve.tensor_copy(small[:, 0:8], PS[:, 0, 16:24]))
                dve.tensor_copy(levelmask[:, :, :, :].rearrange("p a b c -> p (a b c)"), mask_f32)
                mx = small[:, 56:60].rearrange("p (d f) -> p d f", d=2)
                link(dve.tensor_tensor(mx, lbc[:, :, 0, :], lbc[:, :, 1, :], ALU.max))
                ex = small[:, 40:48].rearrange("p (d l f) -> p d l f", d=2, l=DEPTH)
                link(dve.tensor_tensor(ex, lbc, mx.unsqueeze(2).to_broadcast([P, 2, DEPTH, 2]), ALU.subtract))
                dve.wait_ge(s_a, 1)
                link(dve.tensor_tensor(condT[:, :, :].rearrange("p k s -> p s k"),
                                       PS[:, 0, 0:16].rearrange("p (s k) -> p s k", s=2),
                                       small[:, 16:32].rearrange("p (s k) -> p s k", s=2), ALU.mult))
                dve.wait_ge(s_a, 2)
                e = small[:, 48:56].rearrange("p (d l f) -> p d l f", d=2, l=DEPTH)
                link(dve.tensor_tensor(mx, e[:, :, 0, :], e[:, :, 1, :], ALU.add))
                link(dve.reciprocal(mx, mx))
                link(dve.tensor_tensor(e, e, mx.unsqueeze(2).to_broadcast([P, 2, DEPTH, 2]), ALU.mult))
                link(dve.tensor_tensor(lball[:, 0, :, :], e[:, :, 0, :], e[:, :, 0, :], ALU.subtract))
                link(dve.tensor_tensor(lball[:, 1, :, :], e[:, :, 0, :], e[:, :, 1, :], ALU.add))
                link(dve.tensor_tensor(lball[:, 1, :, :], lball[:, 1, :, :], e[:, :, 0, :], ALU.subtract))

        lay_ctx = ExitStack()
        layer_sems = []

        def lsem(name):
            s = lay_ctx.enter_context(nc.semaphore(name))
            layer_sems.append(s)
            return s

        def modulated_norm(name, scale, shift0, buf):
            s_sq, s_ms, s_pw, s_xn, s_tr, s_ev = (lsem(f"{name}_{n}") for n in
                                                  ("squares", "mean", "rstd", "scaled", "turned", "evac"))
            ss, ms, rs = small[:, 64:64 + NT], small[:, 72:72 + NT], small[:, 80:80 + NT]
            with nc.Block() as block:
                @block.scalar
                def _(act):
                    for t in range(NT):
                        if t >= 1:
                            act.wait_ge(s_sq, t)
                        act.activation(buf[:, 0, :], x[:, t, :], ACT.Square,
                                       accum_out=ss[:, t:t + 1]).then_inc(s_sq, 1)
                    act.wait_ge(s_pw, 1)
                    act.wait_ge(s_sq, NT)
                    for t in range(NT):
                        if t >= 2:
                            act.wait_ge(s_tr, t - 1)
                        act.activation(buf[:, t % 2, :], x[:, t, :], ACT.Copy,
                                       scale=rs[:, t:t + 1]).then_inc(s_xn, 1)

                @block.gpsimd
                def _(pool):
                    pool.wait_ge(s_ms, 1)
                    pool.tensor_tensor(rs, ms, minus_half[:, 0:NT], ALU.pow).then_inc(s_pw, 1)

                @block.tensor
                def _(pe):
                    for t in range(NT):
                        pe.wait_ge(s_xn, t + 1)
                        if t >= 2:
                            pe.wait_ge(s_ev, t - 1)
                        for k in range(KC):
                            last = pe.transpose(PS[:, 2 * (t % 2) + k // 4, col(k % 4)], buf[:, t % 2, col(k)], ident)
                        last.then_inc(s_tr, 1)

                @block.vector
                def _(dve):
                    dve.wait_ge(s_sq, NT)
                    dve.tensor_scalar(ms, ss, 1.0 / D, EPS, ALU.mult, ALU.add).then_inc(s_ms, 1)
                    for t in range(NT):
                        dve.wait_ge(s_tr, t + 1)
                        cond = 1 if t else 0
                        for k in range(KC):
                            last = dve.tensor_scalar(hT[:, k, col(t)], PS[:, 2 * (t % 2) + k // 4, col(k % 4)],
                                                     scale[:, k, cond:cond + 1],
                                                     modc[:, shift0 + k, cond:cond + 1], ALU.mult, ALU.add)
                        last.then_inc(s_ev, 1)

        with nc.Fori(0, DEPTH) as layer:
            s_row, s_mw0, s_mw1, s_mr, s_mre, s_mt, s_rowT, s_mv, s_win, s_par = (
                lsem(n) for n in ("rows_load", "modw_load0", "modw_load1", "mod_rows", "mod_rows_evac", "mod_turned",
                                  "rows_turned", "mod_vec", "win_load", "params_load"))
            s_mw = [s_mw0, s_mw1]
            MOD1 = 4
            ck = small[:, 128:384].rearrange("p (s n) -> p s n", s=2)

            def load_mod(sp, n, w):
                if n >= 2 and n != MOD1 and n != MOD1 + 1:
                    sp.wait_ge(s_mr, n - 1)
                sp.dma_start(w[:, n % 2, :, :], mod_w[layer, :, col(n, 512)].rearrange("(k p) n -> p k n", p=P))\
                  .then_inc(s_mw[n % 2], 16)

            def mod_rows(pe, n, w, bank0):
                pe.wait_ge(s_mw[n % 2], 16 * (n // 2 + 1))
                if n >= 2:
                    pe.wait_ge(s_mre, n - 1)
                for k in range(KC):
                    last = pe.matmul(PS[0:2, bank0 + n % 2, :], condT[:, k, :], w[:, n % 2, k, :],
                                     start=(k == 0), stop=(k == KC - 1))
                last.then_inc(s_mr, 1)

            def mod_rows_evac(act, n, dst, bank0):
                act.wait_ge(s_mr, n + 1)
                if n >= 2:
                    act.wait_ge(s_mt, n - 1)
                act.activation(dst[0:2, n % 2, :], PS[0:2, bank0 + n % 2, :], ACT.Copy).then_inc(s_mre, 1)

            def mod_turn(pe, n, src, bank):
                pe.wait_ge(s_mre, n + 1)
                for m in range(4):
                    last = pe.transpose(PS[:, bank, 2 * (4 * n + m):2 * (4 * n + m) + 2], src[0:2, n % 2, col(m)],
                                        ident[0:2, 0:2])
                last.then_inc(s_mt, 1)

            def mod_finish(dve, link, n0, n1, bank, dst, sc0, g0):
                dve.wait_ge(s_mt, n1)
                link(dve.tensor_tensor(modc[:, 4 * n0:4 * n1, :],
                                       PS[:, bank, 8 * n0:8 * n1].rearrange("p (m s) -> p m s", s=2),
                                       small[:, 4 * n0:4 * n1].unsqueeze(2).to_broadcast([P, 4 * (n1 - n0), 2]),
                                       ALU.add))
                link(dve.tensor_scalar(dst[:, :, :], modc[:, sc0:sc0 + KC, :], 1.0, None, ALU.add))
                link(dve.tensor_tensor(dst[:, :, :], dst[:, :, :],
                                       small[:, g0:g0 + KC].unsqueeze(2).to_broadcast([P, KC, 2]), ALU.mult))

            with nc.Block() as block:
                @block.sync
                def _(sp):
                    sp.dma_start(rows[0:48, 0, :], mod_b[layer].rearrange("(a b) -> a b", b=P)).then_inc(s_row, 16)
                    sp.dma_start(rows[0:8, 1, :], norm1_g[layer].rearrange("(a b) -> a b", b=P)).then_inc(s_row, 16)
                    sp.dma_start(rows[0:8, 2, :], norm2_g[layer].rearrange("(a b) -> a b", b=P)).then_inc(s_row, 16)
                    load_mod(sp, 0, modw)
                    load_mod(sp, 1, modw)
                    sp.dma_start(qkg[:, 0, :], q_norm_g[layer].partition_broadcast(P)).then_inc(s_par, 16)
                    sp.dma_start(qkg[:, 1, :], k_norm_g[layer].partition_broadcast(P)).then_inc(s_par, 16)
                    sp.dma_start(ang[:, :], hgrn_norm_g[layer].partition_broadcast(P)).then_inc(s_par, 16)
                    sp.dma_start(sink[:, :], win_sink[layer].partition_broadcast(P)).then_inc(s_par, 16)
                    load_mod(sp, 2, modw)
                    load_mod(sp, 3, modw)
                    for k in range(KC):
                        sp.dma_start(win[:, k, :], w_in[layer, col(k), :]).then_inc(s_win, 16)

                @block.tensor
                def _(pe):
                    pe.wait_ge(s_row, 3 * 16)
                    pe.transpose(PS[:, 3, 0:48], rows[0:48, 0, :], ident[0:48, 0:48])
                    pe.transpose(PS[:, 3, 48:56], rows[0:8, 1, :], ident[0:8, 0:8])
                    pe.transpose(PS[:, 3, 56:64], rows[0:8, 2, :], ident[0:8, 0:8]).then_inc(s_rowT, 1)
                    for n in range(MOD1):
                        mod_rows(pe, n, modw, 0)
                        if n >= 1:
                            mod_turn(pe, n - 1, modrow, 2)
                    mod_turn(pe, MOD1 - 1, modrow, 2)

                @block.scalar
                def _(act):
                    for n in range(MOD1):
                        mod_rows_evac(act, n, modrow, 0)

                @block.vector
                def _(dve):
                    link = chain(dve, s_mv)
                    dve.wait_ge(s_rowT, 1)
                    link(dve.tensor_copy(small[:, 0:64], PS[:, 3, 0:64]))
                    link(dve.tensor_copy(lb[:, :, :], lball[:, bass.ds(layer, 1), :, :].rearrange("p o d f -> p (o d) f")))
                    link(dve.tensor_scalar(olb[:, :, :], lb[:, :, :], -1.0, 1.0, ALU.mult, ALU.add))
                    mod_finish(dve, link, 0, MOD1, 2, scale1, KC, 48)

            modulated_norm("norm1", scale1, 0, xn)

            o_qa, o_ia, o_fa, o_fb, o_ga = 0, AW, 2 * AW, 3 * AW, 4 * AW
            o_qg = 5 * AW
            o_kg, o_vg = o_qg + QW, o_qg + QW + KVW
            o_qw = o_vg + KVW
            o_kw, o_vw = o_qw + QW, o_qw + QW + KVW
            NGRP = 7
            s_z, s_ze, s_zc, s_rd, s_rp, s_rot, s_tp, s_te, s_qs, s_qm, s_cl, s_ct, s_cte, s_co = (
                lsem(n) for n in ("z_done", "z_evac", "qk_vec", "qk_mean", "qk_rstd", "rotated", "z_turned",
                                  "turned_evac_act", "q_sigmoid", "turned_evac_vec", "cache_loaded", "cache_turned",
                                  "cache_evac", "ctx_stored"))
            SG, SW = 768, 1280
            with nc.Block() as block:
                @block.sync
                def _(sp):
                    sp.dma_start(ck[:, 0, :], cgk[0, layer].rearrange("s h d -> s (h d)")).then_inc(s_cl, 16)
                    sp.dma_start(ck[:, 1, :], cwk[0, layer].rearrange("s h d -> s (h d)")).then_inc(s_cl, 16)
                    sp.dma_start(vg[:, NT, :], cgv[0, layer].rearrange("s h d -> s (h d)")).then_inc(s_cl, 16)
                    sp.dma_start(vw[:, NT, :], cwv[0, layer].rearrange("s h d -> s (h d)")).then_inc(s_cl, 16)
                    sp.wait_ge(s_ze, NGRP)
                    sp.dma_start(new_gv[0, layer].rearrange("s h d -> s (h d)"), vg[:, 0, :]).then_inc(s_co, 16)
                    sp.dma_start(new_wv[0, layer].rearrange("s h d -> s (h d)"), vw[:, 0, :]).then_inc(s_co, 16)
                    sp.dma_start(new_wk[0, layer].rearrange("s h d -> s (h d)"),
                                 zs[:, 0, SW + QW:SW + QW + KVW]).then_inc(s_co, 16)
                    sp.wait_ge(s_rot, 1)
                    sp.dma_start(new_gk[0, layer].rearrange("s h d -> s (h d)"),
                                 hT[:, 3, col(0)]).then_inc(s_co, 16)
                    sp.wait_ge(s_co, 4 * 16)

                @block.tensor
                def _(pe):
                    pe.wait_ge(s_cl, 4 * 16)
                    pe.transpose(PS[:, 4, 0:P], ck[:, 0, :], ident)
                    pe.transpose(PS[:, 4, P:2 * P], ck[:, 1, :], ident).then_inc(s_ct, 1)
                    pe.wait_ge(s_win, KC * 16)

                    def turn(t):
                        pe.wait_ge(s_rot, t + 1)
                        pe.wait_ge(s_te, t + 1)
                        if t >= 1:
                            pe.wait_ge(s_qm, 2 * t)
                        for s in range(2):
                            for j in range(4):
                                pe.transpose(PS[:, 4 + s, col(j)], hT[:, 4 * s + j, col(t)], ident)
                        for j in range(6):
                            last = pe.transpose(PS[:, 6 + j // 4, col(j % 4)], zs[:, t % 2, col(j)], ident)
                        last.then_inc(s_tp, 1)

                    grp = 0
                    for t in range(NT):
                        for n in range(NGRP):
                            if grp >= 4:
                                pe.wait_ge(s_ze, grp - 3)
                            for k in range(KC):
                                lhsT = hT[:, k, col(t)]
                                if n in (0, 2):
                                    o = o_qg if n == 0 else o_qw
                                    rhs = win[:, k, o:o + QW].rearrange("p (v j d) -> p j v d", v=KVH, j=G)
                                    out = PS[:, grp % 4, 0:QW].rearrange("p (j v d) -> p j v d", v=KVH, j=G)
                                else:
                                    o, w = {1: (o_kg, 256), 3: (o_kw, 256), 4: (o_fa, 512), 5: (o_qa, 512),
                                            6: (o_ga, 256)}[n]
                                    rhs, out = win[:, k, o:o + w], PS[:, grp % 4, 0:w]
                                last = pe.matmul(out, lhsT, rhs, start=(k == 0), stop=(k == KC - 1))
                            last.then_inc(s_z, 1)
                            grp += 1
                        if t >= 1:
                            turn(t - 1)
                    turn(NT - 1)

                @block.scalar
                def _(act):
                    def turned(t):
                        act.wait_ge(s_tp, t + 1)
                        gates = PS[:, 6, :].rearrange("p (g n) -> p g n", g=4)
                        act.activation(QQ[:, :, col(t)], PS[:, 7, 0:2 * P].rearrange("p (f n) -> p f n", f=2),
                                       ACT.Sigmoid).then_inc(s_qs, 1)
                        act.activation(QF[:, :, :, col(t)].rearrange("p d f n -> p (d f) n"), gates, ACT.Sigmoid)
                        act.activation(KK[:, :, :, col(t)].rearrange("p d f n -> p (d f) n"), gates, ACT.Sigmoid,
                                       scale=-1.0).then_inc(s_te, 1)
                    act.wait_ge(s_ct, 1)
                    act.activation(kT[:, 0, TOK:KEYS], PS[:, 4, 0:P], ACT.Copy)
                    act.activation(kT[:, 1, TOK:KEYS], PS[:, 4, P:2 * P], ACT.Copy).then_inc(s_te, 1)
                    grp = 0
                    for t in range(NT):
                        z = zs[:, t % 2, :]
                        if t >= 2:
                            act.wait_ge(s_tp, t - 1)
                            act.wait_ge(s_rot, t - 1)
                        if t == 2:
                            act.wait_ge(s_co, 4 * 16)
                        for n in range(NGRP):
                            act.wait_ge(s_z, grp + 1)
                            src = PS[:, grp % 4, :]
                            if n == 0:
                                last = act.activation(z[:, SG:SG + QW], src[:, 0:QW], ACT.Copy)
                            elif n == 1:
                                act.activation(z[:, SG + QW:SG + 512], src[:, 0:KVW], ACT.Copy)
                                last = act.activation(vg[:, t, :], src[:, KVW:2 * KVW], ACT.Copy)
                            elif n == 2:
                                last = act.activation(z[:, SW:SW + QW], src[:, 0:QW], ACT.Copy)
                            elif n == 3:
                                act.activation(z[:, SW + QW:SW + 512], src[:, 0:KVW], ACT.Copy)
                                last = act.activation(vw[:, t, :], src[:, KVW:2 * KVW], ACT.Copy)
                            elif n == 4:
                                last = act.activation(z[:, 0:512], src, ACT.Copy)
                            elif n == 5:
                                act.activation(z[:, 512:768], src[:, 0:AW], ACT.Copy)
                                last = act.activation(va[:, t, :], src[:, AW:2 * AW], ACT.Copy)
                            else:
                                last = act.activation(ga[:, t, :], src[:, 0:AW], ACT.Sigmoid)
                            last.then_inc(s_ze, 1)
                            grp += 1
                        if t >= 1:
                            turned(t - 1)
                    turned(NT - 1)

                @block.gpsimd
                def _(pool):
                    for t in range(NT):
                        pool.wait_ge(s_rd, t + 1)
                        pool.tensor_tensor(small[:, 88:96], small[:, 96:104], minus_half[:, 0:8],
                                           ALU.pow).then_inc(s_rp, 1)

                @block.vector
                def _(dve):
                    link = chain(dve, s_zc)
                    ms, rs = small[:, 96:104], small[:, 88:96]

                    def turned(t):
                        dve.wait_ge(s_tp, t + 1)
                        for w in range(2):
                            dve.tensor_copy(qT[:, w, :, col(t)], PS[:, 4 + w, 0:QW].rearrange("p (j n) -> p j n", j=G))
                        dve.tensor_copy(kT[:, :, col(t)], PS[:, 4:6, QW:512]).then_inc(s_qm, 1)
                        dve.wait_ge(s_qs, t + 1)
                        dve.tensor_tensor(QQ[:, :, col(t)], QQ[:, :, col(t)],
                                          PS[:, 7, 0:2 * P].rearrange("p (f n) -> p f n", f=2), ALU.mult)\
                           .then_inc(s_qm, 1)

                    dve.wait_ge(s_par, 4 * 16)
                    for t in range(NT):
                        z = zs[:, t % 2, :]
                        qk = z[:, SG:SG + 512].rearrange("p (c e d) -> p c e d", e=2, d=HD)
                        dst = [hT[:, 4 * s:4 * s + 4, col(t)].rearrange("p c (e d) -> p c e d", d=HD) for s in range(2)]
                        if t >= 1:
                            turned(t - 1)
                        dve.wait_ge(s_ze, NGRP * (t + 1))
                        link(dve.tensor_tensor(dst[0], qk, qk, ALU.mult))
                        link(dve.tensor_reduce(ms, dst[0], AX.X, ALU.add))
                        dve.tensor_scalar(ms, ms, 1.0 / HD, EPS, ALU.mult, ALU.add).then_inc(s_rd, 1)
                        dve.wait_ge(s_rp, t + 1)
                        link(dve.tensor_tensor(qk, qk, rs.rearrange("p (c e) -> p c e", e=2).unsqueeze(3)
                                               .to_broadcast([P, 4, 2, HD]), ALU.mult))
                        out = dst[0] if t == 0 else qk
                        link(dve.tensor_tensor(out[:, 0:3, :, :], qk[:, 0:3, :, :],
                                               qkg[:, 0:1, :].unsqueeze(1).to_broadcast([P, 3, 2, HD]), ALU.mult))
                        link(dve.tensor_tensor(out[:, 3, :, :], qk[:, 3, :, :],
                                               qkg[:, 1:2, :].to_broadcast([P, 2, HD]), ALU.mult))
                        if t == 0:
                            dve.tensor_copy(hT[:, 4:8, col(0)], z[:, SW:SW + 512].rearrange("p (c n) -> p c n", c=4))\
                               .then_inc(s_rot, 1)
                            continue
                        for s, base in ((0, SG), (1, SW)):
                            src = z[:, base:base + 512].rearrange("p (c m b f) -> p c m b f", c=4, m=4, b=2)
                            o = hT[:, 4 * s:4 * s + 4, col(t)].rearrange("p c (m b f) -> p c m b f", m=4, b=2)
                            cs = cosT[:, t - 1:t, :, :].to_broadcast([P, 4, 4, 16])
                            sn = sinT[:, t - 1:t, :, :].to_broadcast([P, 4, 4, 16])
                            x1, x2 = src[:, :, :, 0, :], src[:, :, :, 1, :]
                            o1, o2 = o[:, :, :, 0, :], o[:, :, :, 1, :]
                            dve.tensor_tensor(o1, x1, cs, ALU.mult)
                            link(dve.tensor_tensor(o2, x2, cs, ALU.mult))
                            dve.tensor_tensor(x2, x2, sn, ALU.mult)
                            link(dve.tensor_tensor(x1, x1, sn, ALU.mult))
                            dve.tensor_tensor(o1, o1, x2, ALU.subtract)
                            ins = dve.tensor_tensor(o2, o2, x1, ALU.add)
                            if s == 1:
                                ins.then_inc(s_rot, 1)
                            else:
                                link(ins)
                    turned(NT - 1)

            s_hv, s_hm, s_hs, s_he, s_wo, s_hg, s_st, s_hk, s_hke, s_ho, s_hd, s_hS, s_hx, s_hp, s_hq, s_so = (
                lsem(n) for n in ("scan_vec", "scan_products", "scan_scores", "scan_scores_evac", "wout_load",
                                  "scan_pool", "state_load", "kout_turned", "kout_evac", "scan_out", "state_step_pe",
                                  "state_step", "scan_sq", "scan_mean", "scan_rstd", "state_stored"))
            NLEV = len(LEVELS) + 1
            STATE_STEPS = [(0, 0, None), (1, 0, None)] + [(d, i + 1 if d == 0 else NL - i, i)
                                                          for d in range(2) for i in range(NL - 1)]
            with nc.Block() as block:
                @block.sync
                def _(sp):
                    load_mod(sp, MOD1, modw2)
                    load_mod(sp, MOD1 + 1, modw2)
                    sp.wait_ge(s_hg, 1)
                    for d in range(2):
                        step = 0
                        for h in range(AH):
                            f, r = h // 2, h % 2
                            sp.dma_start(Sv[64 * r:64 * r + 64, d, step, f, 64 * r:64 * r + 64],
                                         state[0, layer, d, h]).then_inc(s_st, 16)
                    for n in range(MOD1 + 2, 12):
                        load_mod(sp, n, modw2)
                    sp.wait_ge(s_hS, 2)
                    for d in range(2):
                        for h in range(AH):
                            f, r = h // 2, h % 2
                            sp.dma_start(new_state[0, layer, d, h], Sc[64 * r:64 * r + 64, d, f, :])\
                              .then_inc(s_so, 16)
                    sp.wait_ge(s_so, 8 * 16)

                @block.gpsimd
                def _(pool):
                    pool.memset(Sv, 0.0).then_inc(s_hg, 1)
                    pool.memset(KF, 1.0).then_inc(s_hg, 1)
                    pool.memset(Am, 0.0).then_inc(s_hg, 1)
                    pool.wait_ge(s_hp, 1)
                    pool.tensor_tensor(small[:, 88:88 + NT * AH], small[:, 112:112 + NT * AH],
                                       minus_half[:, 0:NT * AH], ALU.pow).then_inc(s_hq, 1)

                @block.tensor
                def _(pe):
                    unit = 0
                    for lv in range(NLEV):
                        for d in range(2):
                            pe.wait_ge(s_hm, 2 * lv + d + 1)
                            for t in range(NT):
                                if unit >= 2:
                                    pe.wait_ge(s_he, unit - 1)
                                for h in range(AH):
                                    f, r = h // 2, h % 2
                                    k_op = KK if lv == 0 else M
                                    rhs = QQ[64 * r:64 * r + 64, f, col(t)] if lv == 0 else \
                                        M[64 * r:64 * r + 64, d, f, col(t)]
                                    last = pe.matmul(PS[:, 2 * (unit % 2) + r, col(f)],
                                                     k_op[64 * r:64 * r + 64, d, f, col(t)], rhs,
                                                     start=True, stop=True)
                                last.then_inc(s_hs, 1)
                                unit += 1
                            n = MOD1 + lv
                            if d == 0 and n < 12:
                                mod_rows(pe, n, modw2, 4)
                            elif n < 12:
                                mod_turn(pe, n, modrow2, 6)
                    pe.wait_ge(s_hm, 2 * NLEV + 1)
                    pe.wait_ge(s_he, 2 * NLEV * NT)
                    for n, (d, t, step) in enumerate(STATE_STEPS):
                        if n >= 2:
                            pe.wait_ge(s_hke, n - 1)
                        for f in range(2):
                            last = pe.transpose(PS[:, n % 2, col(f)], KK[:, d, f, col(t)], ident)
                        last.then_inc(s_hk, 1)
                        pe.wait_ge(s_hke, n + 1)
                        if n >= 1:
                            pe.wait_ge(s_hS, n)
                        for f in range(2):
                            last = pe.matmul(PS[:, 2, col(f)], kout[:, n % 2, col(f)], va[:, t, col(f)],
                                             start=True, stop=True)
                        last.then_inc(s_hd, 1)
                    pe.wait_ge(s_hS, len(STATE_STEPS))
                    for t in range(NT):
                        o = PS[:, 3 + t, :]
                        first = True
                        for d in range(2):
                            if t > 0:
                                step = t - 1 if d == 0 else NL - t
                                for f in range(2):
                                    pe.matmul(o[:, col(f)], M[:, d, f, col(t)], Sv[:, d, step, f, :],
                                              start=first, stop=False, skip_group_check=True)
                                    first = False
                            for h in range(AH):
                                f, r = h // 2, h % 2
                                last = pe.matmul(o[:, h * HD:(h + 1) * HD], Am[:, d, t, 2 * r + f, :],
                                                 va[:, t, h * HD:(h + 1) * HD], start=first,
                                                 stop=(d == 1 and h == AH - 1), skip_group_check=True)
                                first = False
                        last.then_inc(s_ho, 1)

                @block.scalar
                def _(act):
                    for n in range(MOD1, 12):
                        mod_rows_evac(act, n, modrow2, 4)
                    for n in range(len(STATE_STEPS)):
                        act.wait_ge(s_hk, n + 1)
                        if n >= 2:
                            act.wait_ge(s_hd, n - 1)
                        act.activation(kout[:, n % 2, :], PS[:, n % 2, 0:AW], ACT.Copy).then_inc(s_hke, 1)
                    for t in range(NT):
                        act.wait_ge(s_ho, t + 1)
                        act.activation(osq[:, t, :], PS[:, 3 + t, 0:AW], ACT.Square).then_inc(s_hx, 1)

                @block.vector
                def _(dve):
                    link = chain(dve, s_hv)
                    dve.wait_ge(s_hg, 3)
                    for d in range(2):
                        for f in range(2):
                            link(dve.tensor_scalar(QF[:, d, f, :], QF[:, d, f, :], olb[:, d, f:f + 1],
                                                   lb[:, d, f:f + 1], ALU.mult, ALU.add))
                            link(dve.tensor_scalar(QF[:, d, f, :], QF[:, d, f, :], TINY, None, ALU.max))
                            ins = dve.tensor_scalar(KK[:, d, f, :], KK[:, d, f, :], olb[:, d, f:f + 1], None, ALU.mult)
                        ins.then_inc(s_hm, 1)
                    dve.wait_ge(s_hm, 2)
                    qq = QQ.rearrange("p f n -> p (f n)")

                    def evac(lv, d):
                        for t in range(NT):
                            unit = (2 * lv + d) * NT + t
                            dve.wait_ge(s_hs, unit + 1)
                            dve.copy_predicated(
                                Am[:, d, t, :, :],
                                levelmask[:, d, lv, :].unsqueeze(1).to_broadcast([P, 4, P]),
                                PS[:, 2 * (unit % 2):2 * (unit % 2) + 2, 0:2 * P]).then_inc(s_he, 1)

                    evac(0, 0)
                    evac(0, 1)
                    for lv, h in enumerate(LEVELS, start=1):
                        for d in range(2):
                            qs, ks = (1, 0) if d == 0 else (0, 1)
                            last_pos = h - 1 if d == 0 else 0
                            nb = 2 * TOK // (2 * h)

                            def blocks(a):
                                return a.rearrange("p (n two h) -> p n two h", two=2, h=h)

                            m, q, kk, qf, kf = (blocks(a) for a in (
                                M[:, d, :, :].rearrange("p f n -> p (f n)"), qq,
                                KK[:, d, :, :].rearrange("p f n -> p (f n)"),
                                QF[:, d, :, :].rearrange("p f n -> p (f n)"),
                                KF[:, d, :, :].rearrange("p f n -> p (f n)")))

                            def block_product(side):
                                return qf[:, :, side, last_pos:last_pos + 1].to_broadcast([P, nb, h])

                            dve.wait_ge(s_hs, (2 * (lv - 1) + d + 1) * NT)
                            dve.tensor_tensor(m[:, :, qs, :], q[:, :, qs, :], qf[:, :, qs, :], ALU.mult)
                            dve.tensor_tensor(m[:, :, ks, :], kk[:, :, ks, :], kf[:, :, ks, :], ALU.mult)\
                               .then_inc(s_hm, 1)
                            dve.wait_ge(s_hm, 2 * lv + d + 1)
                            link(dve.tensor_tensor(kf[:, :, ks, :], kf[:, :, ks, :], block_product(qs), ALU.mult))
                            link(dve.tensor_tensor(qf[:, :, qs, :], qf[:, :, qs, :], block_product(ks), ALU.mult))
                        evac(lv, 0)
                        evac(lv, 1)
                    for d in range(2):
                        dve.tensor_tensor(M[:, d, :, :], QQ, QF[:, d, :, :], ALU.mult)
                        ins = dve.tensor_tensor(KK[:, d, :, :], KK[:, d, :, :], KF[:, d, :, :], ALU.mult)
                    ins.then_inc(s_hm, 1)
                    mod_finish(dve, link, MOD1, 12, 6, scale2, 4 * KC, 56)
                    dve.wait_ge(s_st, 8 * 16)
                    for n, (d, t, step) in enumerate(STATE_STEPS):
                        dve.wait_ge(s_hd, n + 1)
                        edge = t * P + (P - 1 if d == 0 else 0)
                        if n >= 1:
                            dve.wait_ge(s_hS, n)
                        for r in range(2):
                            rows_r = slice(64 * r, 64 * r + 64)
                            if t == 0:
                                ins = dve.tensor_copy(Sc[rows_r, d, :, :],
                                                      PS[rows_r, 2, 0:2 * P].rearrange("p (f n) -> p f n", f=2)
                                                      [:, :, 64 * r:64 * r + 64])
                                continue
                            for f in range(2):
                                ins = dve.scalar_tensor_tensor(
                                    Sv[rows_r, d, step + 1, f, rows_r], Sv[rows_r, d, step, f, rows_r],
                                    QF[rows_r, d, f, edge:edge + 1],
                                    PS[rows_r, 2, f * P + 64 * r:f * P + 64 * r + 64], ALU.mult, ALU.add)
                        ins.then_inc(s_hS, 1)
                    ms = small[:, 112:112 + NT * AH]
                    rs = small[:, 88:88 + NT * AH].rearrange("p (t a) -> p t a", t=NT)
                    dve.wait_ge(s_hx, NT)
                    link(dve.tensor_reduce(ms, osq.rearrange("p t (a d) -> p (t a) d", d=HD), AX.X, ALU.add))
                    dve.tensor_scalar(ms, ms, 1.0 / HD, EPS, ALU.mult, ALU.add).then_inc(s_hp, 1)
                    dve.wait_ge(s_hq, 1)
                    for t in range(NT):
                        dst = oall[:, t, 0:AW].rearrange("p (a d) -> p a d", d=HD)
                        link(dve.tensor_tensor(dst, PS[:, 3 + t, 0:AW].rearrange("p (a d) -> p a d", d=HD),
                                               rs[:, t, :].unsqueeze(2).to_broadcast([P, AH, HD]), ALU.mult))
                        link(dve.tensor_tensor(dst, dst, ang[:, :].unsqueeze(1).to_broadcast([P, AH, HD]), ALU.mult))
                        link(dve.tensor_tensor(oall[:, t, 0:AW], oall[:, t, 0:AW], ga[:, t, :], ALU.mult))

            s_as, s_am, s_ax, s_at, s_acv, s_aca, s_apv, s_aev, s_ach, s_es, s_esx = (
                lsem(n) for n in ("att_scores", "att_bias", "att_exp", "att_turned", "att_copy_vec", "att_copy_act",
                                  "att_pv", "att_out", "att_vec", "sink_shifted", "sink_exp"))
            units = []
            for t in range(NT):
                for wnd in range(2):
                    if t == 0:
                        keys, moff = [0], None
                    elif not wnd:
                        keys, moff = list(range(1, NT + 1)), None
                    else:
                        keys = ([t - 1] if t > 1 else []) + [t, NT] + ([t + 1] if t < NL else [])
                        moff = 0 if t > 1 else P
                    for j in range(G):
                        for kv in range(KVH):
                            units.append((t, wnd, kv, j, keys, moff))
            U = len(units)
            groups = U // QH
            negsink = small[:, 136:142]
            nbias = small[:, 144:144 + U]
            rsum = small[:, 208:208 + U]
            rinv = small[:, 272:272 + U]
            mxs = small[:, 336:336 + U]
            eshift = small[:, 400:412].rearrange("p (s h) -> p s h", s=2)
            esx = small[:, 416:428].rearrange("p (s h) -> p s h", s=2)

            def unit_head(u):
                return units[u][2] * G + units[u][3]

            first_half = [(len(un[4]) + 1) // 2 for un in units]
            act_copies = [sum(len(un[4]) > 1 for un in units[:u]) for u in range(U + 1)]

            def stat(a, u):
                n = (u // QH) * QH + unit_head(u)
                return a[:, n:n + 1]

            with nc.Block() as block:
                @block.sync
                def _(sp):
                    sp.dma_start(wout[:, :, :], w_out[layer].rearrange("(k p) n -> p k n", p=P)).then_inc(s_wo, 16)

                @block.tensor
                def _(pe):
                    def scores(u):
                        t, wnd, kv, j, keys, _ = units[u]
                        if u >= 2:
                            pe.wait_ge(s_ax, u - 1)
                        kv_rows = slice(64 * kv, 64 * kv + 64)
                        runs = []
                        for n, kt in enumerate(keys):
                            if runs and runs[-1][1] + runs[-1][2] == kt and n % 4:
                                runs[-1][2] += 1
                            else:
                                runs.append([n, kt, 1])
                        for n, kt, m in runs:
                            last = pe.matmul(PS[:, 2 * (u % 2) + n // 4, (n % 4) * P:(n % 4 + m) * P],
                                             qT[kv_rows, wnd, j, col(t)], kT[kv_rows, wnd, kt * P:(kt + m) * P],
                                             start=True, stop=True)
                        last.then_inc(s_as, 1)

                    def turn(u):
                        pe.wait_ge(s_ax, u + 1)
                        if u >= 1:
                            pe.wait_ge(s_acv, u)
                            if act_copies[u]:
                                pe.wait_ge(s_aca, act_copies[u])
                        for n in range(len(units[u][4])):
                            bank, at = (4, n) if n < first_half[u] else (5, n - first_half[u])
                            last = pe.transpose(PS[:, bank, col(at)], pr[:, u % 2, col(n)], ident)
                        last.then_inc(s_at, 1)

                    def weigh(u):
                        t, wnd, kv, j, keys, _ = units[u]
                        pe.wait_ge(s_acv, u + 1)
                        if act_copies[u + 1]:
                            pe.wait_ge(s_aca, act_copies[u + 1])
                        g = u // QH
                        if u % QH == 0 and g >= 2:
                            pe.wait_ge(s_aev, g - 1)
                        h = unit_head(u)
                        v = vw if wnd else vg
                        for n, kt in enumerate(keys):
                            last = pe.matmul(PS[:, 6 + g % 2, h * HD:(h + 1) * HD], prT[:, u % 2, col(n)],
                                             v[:, kt, kv * HD:(kv + 1) * HD], start=(n == 0), stop=(n == len(keys) - 1))
                        last.then_inc(s_apv, 1)

                    for step in range(U + 2):
                        if step < U:
                            scores(step)
                        if 1 <= step <= U:
                            turn(step - 1)
                        if step >= 2:
                            weigh(step - 2)

                @block.scalar
                def _(act):
                    for step in range(U + 1):
                        if step < U:
                            u = step
                            t, wnd, kv, j, keys, moff = units[u]
                            n = len(keys) * P
                            act.wait_ge(s_am, u + 1)
                            if u >= 2:
                                act.wait_ge(s_at, u - 1)
                            src = PS[:, 2 * (u % 2):2 * (u % 2) + 2, :].rearrange("p b n -> p (b n)")[:, 0:n]
                            if moff is not None:
                                src = sm[:, u % 2, 0:n]
                            act.activation(pr[:, u % 2, 0:n], src, ACT.Exp, bias=stat(nbias, u), scale=SCALE,
                                           accum_out=stat(rsum, u)).then_inc(s_ax, 1)
                            if u % QH == QH - 1 and wnd:
                                act.wait_ge(s_es, u // QH // 2 + 1)
                                act.activation(esx[:, (u // QH // 2) % 2, :], eshift[:, (u // QH // 2) % 2, :],
                                               ACT.Exp).then_inc(s_esx, 1)
                        if step >= 1 and len(units[step - 1][4]) > 1:
                            u = step - 1
                            n, m = len(units[u][4]) * P, first_half[u] * P
                            act.wait_ge(s_at, u + 1)
                            if u >= 2:
                                act.wait_ge(s_apv, u - 1)
                            act.activation(prT[:, u % 2, m:n], PS[:, 5, 0:n - m], ACT.Copy).then_inc(s_aca, 1)

                @block.vector
                def _(dve):
                    link = chain(dve, s_ach)
                    link(dve.tensor_scalar(negsink, sink[:, :], -1.0, None, ALU.mult))
                    for step in range(U + 3):
                        if step < U:
                            u = step
                            t, wnd, kv, j, keys, moff = units[u]
                            n = len(keys) * P
                            h = unit_head(u)
                            src = PS[:, 2 * (u % 2):2 * (u % 2) + 2, :].rearrange("p b n -> p (b n)")[:, 0:n]
                            dve.wait_ge(s_as, u + 1)
                            if moff is None:
                                link(dve.tensor_reduce(stat(mxs, u), src, AX.X, ALU.max))
                            else:
                                if u >= 2:
                                    dve.wait_ge(s_ax, u - 1)
                                link(dve.tensor_tensor_reduce(sm[:, u % 2, 0:n], src, winmask[:, moff:moff + n],
                                                              1.0, 0.0, ALU.add, ALU.max, stat(mxs, u)))
                            if wnd:
                                dve.tensor_scalar(stat(nbias, u), stat(mxs, u), -SCALE, negsink[:, h:h + 1],
                                                  ALU.mult, ALU.min).then_inc(s_am, 1)
                            else:
                                dve.tensor_scalar(stat(nbias, u), stat(mxs, u), -SCALE, None, ALU.mult)\
                                   .then_inc(s_am, 1)
                            if u % QH == QH - 1 and wnd:
                                g = u // QH
                                dve.wait_ge(s_am, u + 1)
                                dve.tensor_tensor(eshift[:, (g // 2) % 2, :], nbias[:, g * QH:(g + 1) * QH],
                                                  sink[:, :], ALU.add).then_inc(s_es, 1)
                        if 1 <= step <= U:
                            u = step - 1
                            m = first_half[u] * P
                            dve.wait_ge(s_at, u + 1)
                            if u >= 2:
                                dve.wait_ge(s_apv, u - 1)
                            dve.tensor_copy(prT[:, u % 2, 0:m], PS[:, 4, 0:m]).then_inc(s_acv, 1)
                        if step >= 3 and (step - 3) % QH == QH - 1:
                            g = (step - 3) // QH
                            t, wnd = units[step - 3][0:2]
                            den = rsum[:, g * QH:(g + 1) * QH]
                            inv = rinv[:, g * QH:(g + 1) * QH]
                            dve.wait_ge(s_apv, (g + 1) * QH)
                            if wnd:
                                dve.wait_ge(s_esx, g // 2 + 1)
                                link(dve.tensor_tensor(inv, den, esx[:, (g // 2) % 2, :], ALU.add))
                                link(dve.reciprocal(inv, inv))
                            else:
                                link(dve.reciprocal(inv, den))
                            o0 = AW + wnd * QW
                            dve.tensor_tensor(oall[:, t, o0:o0 + QW].rearrange("p (h d) -> p h d", d=HD),
                                              PS[:, 6 + g % 2, 0:QW].rearrange("p (h d) -> p h d", d=HD),
                                              inv.unsqueeze(2).to_broadcast([P, QH, HD]), ALU.mult)\
                               .then_inc(s_aev, 1)

            s_gb, s_gbe, s_ot, s_ote, s_y, s_yp, s_yv = (
                lsem(n) for n in ("gate_rows", "gate_rows_evac", "o_turned", "o_turned_evac", "y_done", "y_gated",
                                  "y_added"))

            def gate_rows(pe, columns, bank0, s_sig):
                for cond in range(2):
                    for k in range(KC):
                        last = pe.matmul(PS[:, bank0 + 2 * cond + k // 4, col(k % 4)],
                                         columns[:, k, cond:cond + 1].to_broadcast([P, P]), ident,
                                         start=True, stop=True)
                last.then_inc(s_sig, 1)

            with nc.Block() as block:
                @block.tensor
                def _(pe):
                    gate_rows(pe, modc[:, 2 * KC:3 * KC, :], 4, s_gb)
                    pe.wait_ge(s_wo, 16)

                    def turn(t):
                        if t >= 2:
                            pe.wait_ge(s_ote, t - 1)
                        for k in range(KC):
                            last = pe.transpose(PS[:, 2 * (t % 2) + k // 4, col(k % 4)], oall[:, t, col(k)], ident)
                        last.then_inc(s_ot, 1)

                    turn(0)
                    for t in range(NT):
                        if t + 1 < NT:
                            turn(t + 1)
                        pe.wait_ge(s_ote, t + 1)
                        if t < 2:
                            pe.wait_ge(s_gbe, 1)
                        else:
                            pe.wait_ge(s_yp, t - 1)
                        for b in range(2):
                            for k in range(KC):
                                last = pe.matmul(PS[:, 4 + 2 * (t % 2) + b, :], oT[:, t % 2, k, :],
                                                 wout[:, k, col(b, 512)], start=(k == 0), stop=(k == KC - 1))
                        last.then_inc(s_y, 1)

                @block.scalar
                def _(act):
                    act.wait_ge(s_gb, 1)
                    act.activation(g1b[:, :, :].rearrange("p s n -> p (s n)"),
                                   PS[:, 4:8, :].rearrange("p b n -> p (b n)"), ACT.Copy).then_inc(s_gbe, 1)
                    for t in range(NT):
                        act.wait_ge(s_ot, t + 1)
                        if t >= 2:
                            act.wait_ge(s_y, t - 1)
                        act.activation(oT[:, t % 2, :, :].rearrange("p k n -> p (k n)"),
                                       PS[:, 2 * (t % 2):2 * (t % 2) + 2, :].rearrange("p b n -> p (b n)"),
                                       ACT.Copy).then_inc(s_ote, 1)

                @block.vector
                def _(dve):
                    dve.wait_ge(s_gbe, 1)
                    for t in range(NT):
                        dve.wait_ge(s_y, t + 1)
                        if t >= 2:
                            dve.wait_ge(s_yv, t - 1)
                        dve.tensor_tensor(prod[:, t % 2, :],
                                          PS[:, 4 + 2 * (t % 2):6 + 2 * (t % 2), :].rearrange("p b n -> p (b n)"),
                                          g1b[:, 1 if t else 0, :], ALU.mult).then_inc(s_yp, 1)
                        dve.wait_ge(s_yp, t + 1)
                        dve.tensor_tensor(x[:, t, :], x[:, t, :], prod[:, t % 2, :], ALU.add).then_inc(s_yv, 1)

            (s_n2q, s_n2m, s_n2p, s_n2x, s_n2r, s_n2e, s_n2h, s_n2t, s_n2c, s_hst, s_rw, s_rl, s_rg, s_rv, s_cnt,
             s_sz, s_sc, s_sl, s_rdy) = (
                lsem(n) for n in ("norm2_squares", "norm2_mean", "norm2_rstd", "norm2_scaled", "rows_made",
                                  "rows_evac", "norm2_rows", "norm2_turned", "norm2_turned_evac", "h_stored",
                                  "router_load", "router_logits", "router_sigmoid", "router_vec", "pair_counts",
                                  "slots_zeroed", "slots_scattered", "slots_loaded", "slots_ready"))
            ss, ms, rs = small[:, 64:64 + NT], small[:, 72:72 + NT], small[:, 80:80 + NT]
            nte = NT * NE
            sc, sel = rt[:, 0:nte], rt[:, nte:2 * nte]
            rk, top2, tv = (rt[:, 240 + nte * n:240 + nte * (n + 1)] for n in range(3))
            gs, grk, gm = (rt[:, 520 + 20 * n:540 + 20 * n] for n in range(3))
            den, inv = rt[:, 600:605], rt[:, 608:613]
            before = rc[:, RC_BEFORE:RC_BEFORE + P]
            all_ones = rc[:, RC_ONES:RC_ONES + P]

            def by_expert(a):
                return a.rearrange("p (t e) -> p t e", e=NE)

            with nc.Block() as block:
                @block.sync
                def _(sp):
                    sp.dma_start(rw, router_w.rearrange("(k p) n -> p k n", p=P)).then_inc(s_rw, 16)
                    sp.dma_start(rc, route_consts).then_inc(s_rw, 16)
                    for t in range(NT):
                        sp.wait_ge(s_n2h, 2 * t + 2)
                        sp.dma_start(h_dram[col(t), :], h2[:, t, :]).then_inc(s_hst, 16)
                    sp.wait_ge(s_hst, NT * 16)

                @block.gpsimd
                def _(pool):
                    pool.memset(zero_i, 0).then_inc(s_sz, 1)
                    pool.wait_ge(s_sz, 1)
                    pool.dma_start(slot_dram.rearrange("(p n) o -> p (n o)", p=P), zero_i).then_inc(s_sc, 16)
                    pool.wait_ge(s_n2m, 1)
                    pool.tensor_tensor(rs, ms, minus_half[:, 0:NT], ALU.pow).then_inc(s_n2p, 1)
                    pool.wait_ge(s_rdy, 1)
                    pool.wait_ge(s_sc, 16)
                    for t in range(NT):
                        for cc in range(2):
                            pool.indirect_dma_start(
                                out=slot_dram, out_offset=bass.IndirectOffsetOnAxis(slot_i[:, cc, t:t + 1], 0),
                                in_=token_i[:, t:t + 1], in_offset=None).then_inc(s_sc, 16)
                    pool.wait_ge(s_sc, 16 + 2 * NT * 16)
                    pool.dma_start(slot_token, slot_dram.rearrange("(t p) o -> p (t o)", p=P),
                                   allow_slow_non_contiguous=True).then_inc(s_sl, 16)
                    pool.wait_ge(s_sl, 16)

                @block.scalar
                def _(act):
                    for t in range(NT):
                        if t >= 1:
                            act.wait_ge(s_n2q, t)
                        act.activation(h2[:, NT - 1, :], x[:, t, :], ACT.Square,
                                       accum_out=ss[:, t:t + 1]).then_inc(s_n2q, 1)
                    act.wait_ge(s_n2p, 1)
                    act.wait_ge(s_n2q, NT)
                    for t in range(NT):
                        act.activation(h2[:, t, :], x[:, t, :], ACT.Copy, scale=rs[:, t:t + 1]).then_inc(s_n2x, 1)
                    for t in range(NT):
                        act.wait_ge(s_n2t, t + 1)
                        act.activation(hT[:, :, col(t)],
                                       PS[:, 2 * (t % 2):2 * (t % 2) + 2, :].rearrange("p b (k n) -> p (b k) n", k=4),
                                       ACT.Copy).then_inc(s_n2c, 1)
                    act.wait_ge(s_rl, 1)
                    act.activation(sc, PS[:, 4, 0:nte], ACT.Sigmoid).then_inc(s_rg, 1)

                @block.tensor
                def _(pe):
                    gate_rows(pe, scale2[:, :, :], 4, s_n2r)
                    gate_rows(pe, modc[:, 3 * KC:4 * KC, :], 0, s_n2r)
                    pe.wait_ge(s_n2e, 1)
                    gate_rows(pe, modc[:, 5 * KC:6 * KC, :], 4, s_n2r)
                    pe.wait_ge(s_n2e, 3)
                    pe.wait_ge(s_rw, 2 * 16)
                    for t in range(NT + 1):
                        if t < NT:
                            pe.wait_ge(s_n2h, 2 * t + 2)
                            if t >= 2:
                                pe.wait_ge(s_n2c, t - 1)
                            for k in range(KC):
                                last = pe.transpose(PS[:, 2 * (t % 2) + k // 4, col(k % 4)], h2[:, t, col(k)], ident)
                            last.then_inc(s_n2t, 1)
                        if t >= 1:
                            pe.wait_ge(s_n2c, t)
                            for k in range(KC):
                                last = pe.matmul(PS[:, 4, (t - 1) * NE:t * NE], hT[:, k, col(t - 1)], rw[:, k, :],
                                                 start=(k == 0), stop=(k == KC - 1))
                    last.then_inc(s_rl, 1)
                    pe.wait_ge(s_cnt, 1)
                    for t in range(NT):
                        for q in range(t):
                            pe.matmul(PS[:, 5, t * NE:(t + 1) * NE], all_ones, by_expert(top2)[:, q, :],
                                      start=(q == 0), stop=False)
                        pe.matmul(PS[:, 5, t * NE:(t + 1) * NE], before, by_expert(top2)[:, t, :],
                                  start=(t == 0), stop=True)
                    for q in range(NT):
                        last = pe.matmul(PS[:, 5, nte:nte + NE], all_ones, by_expert(top2)[:, q, :],
                                         start=(q == 0), stop=(q == NT - 1))
                    last.then_inc(s_rl, 1)

                @block.vector
                def _(dve):
                    link = chain(dve, s_rv)
                    for n, (dst, bank0) in enumerate(((arow, 4), (brow, 0), (g2b, 4))):
                        dve.wait_ge(s_n2r, n + 1)
                        dve.tensor_copy(dst.rearrange("p s n -> p (s n)"),
                                        PS[:, bank0:bank0 + 4, :].rearrange("p b n -> p (b n)")).then_inc(s_n2e, 1)
                        if n == 1:
                            dve.wait_ge(s_n2q, NT)
                            dve.tensor_scalar(ms, ss, 1.0 / D, EPS, ALU.mult, ALU.add).then_inc(s_n2m, 1)
                    dve.wait_ge(s_n2e, 3)
                    for t in range(NT):
                        cond = 1 if t else 0
                        dve.wait_ge(s_n2x, t + 1)
                        dve.tensor_tensor(h2[:, t, :], h2[:, t, :], arow[:, cond, :], ALU.mult).then_inc(s_n2h, 1)
                        dve.wait_ge(s_n2h, 2 * t + 1)
                        dve.tensor_tensor(h2[:, t, :], h2[:, t, :], brow[:, cond, :], ALU.add).then_inc(s_n2h, 1)

                    def rank(out, val, n):
                        def four(a):
                            return a.rearrange("p (n i j) -> p n i j", i=4, j=4)
                        other = val.rearrange("p (n j) -> p n j", j=4).unsqueeze(2).to_broadcast([P, n, 4, 4])
                        mine = val.rearrange("p (n j) -> p n j", j=4).unsqueeze(3).to_broadcast([P, n, 4, 4])
                        gt, eq = rt[:, 1024:1024 + 16 * n], rt[:, 2048:2048 + 16 * n]
                        dve.tensor_tensor(four(gt), other, mine, ALU.is_gt)
                        link(dve.tensor_tensor(four(eq), other, mine, ALU.is_equal))
                        link(dve.tensor_tensor(eq.rearrange("p (n k) -> p n k", k=16), eq.rearrange("p (n k) -> p n k", k=16),
                                               ltmask.unsqueeze(1).to_broadcast([P, n, 16]), ALU.mult))
                        link(dve.tensor_tensor(gt, gt, eq, ALU.add))
                        link(dve.tensor_reduce(out, gt.rearrange("p (m j) -> p m j", j=4), AX.X, ALU.add))

                    dve.wait_ge(s_rg, 1)
                    link(dve.tensor_tensor(by_expert(sel), by_expert(sc),
                                           rbias[:, :].unsqueeze(1).to_broadcast([P, NT, NE]), ALU.add))
                    rank(rk, sel, NT * NG)
                    link(dve.tensor_scalar(top2, rk, 2.0, None, ALU.is_lt))
                    link(dve.tensor_tensor(tv, sel, top2, ALU.mult))
                    link(dve.tensor_reduce(gs, tv.rearrange("p (m j) -> p m j", j=EPG), AX.X, ALU.add))
                    rank(grk, gs, NT)
                    link(dve.tensor_scalar(gm, grk, 1.0, None, ALU.is_lt))
                    dve.tensor_tensor(top2.rearrange("p (m j) -> p m j", j=EPG),
                                      top2.rearrange("p (m j) -> p m j", j=EPG),
                                      gm.unsqueeze(2).to_broadcast([P, NT * NG, EPG]), ALU.mult).then_inc(s_cnt, 1)
                    dve.wait_ge(s_cnt, 1)
                    link(dve.tensor_tensor(tv, sc, top2, ALU.mult))
                    link(dve.tensor_reduce(den, by_expert(tv), AX.X, ALU.add))
                    link(dve.reciprocal(inv, den))
                    link(dve.tensor_tensor(by_expert(tv), by_expert(tv), inv.unsqueeze(2).to_broadcast([P, NT, NE]),
                                           ALU.mult))
                    cnt, nt, end, base, on = (rt[:, 640 + 16 * n:656 + 16 * n] for n in range(5))
                    slots, tmp = rt[:, 720:720 + nte], rt[:, 800:800 + nte]
                    dve.wait_ge(s_rl, 2)
                    link(dve.tensor_copy(cnt, PS[:, 5, nte:nte + NE]))
                    link(dve.tensor_scalar(nt, cnt, 0.0, None, ALU.is_gt))
                    for m in range(1, NT):
                        link(dve.scalar_tensor_tensor(nt, cnt, float(P * m), nt, ALU.is_gt, ALU.add))
                    link(dve.memset(on, 1.0))
                    link(dve.tensor_tensor_scan(end, on, nt, 0.0, ALU.mult, ALU.add))
                    link(dve.tensor_tensor(base, end, nt, ALU.subtract))
                    link(dve.tensor_scalar(base, base, float(P), None, ALU.mult))
                    link(dve.tensor_tensor(by_expert(slots), PS[:, 5, 0:nte].rearrange("p (t e) -> p t e", e=NE),
                                           base.unsqueeze(1).to_broadcast([P, NT, NE]), ALU.add))
                    link(dve.scalar_tensor_tensor(tmp, slots, 1.0, top2, ALU.add, ALU.mult))
                    link(dve.tensor_reduce(slot_f[:, 0, :], by_expert(tmp), AX.X, ALU.max))
                    link(dve.tensor_scalar(slot_f[:, 0, :], slot_f[:, 0, :], -1.0, None, ALU.add))
                    far = float(NS * P)
                    link(dve.tensor_scalar(tmp, slots, -1.0, far, ALU.mult, ALU.add))
                    link(dve.tensor_tensor(tmp, tmp, top2, ALU.mult))
                    link(dve.tensor_reduce(slot_f[:, 1, :], by_expert(tmp), AX.X, ALU.max))
                    link(dve.tensor_scalar(slot_f[:, 1, :], slot_f[:, 1, :], -1.0, far, ALU.mult, ALU.add))
                    for cc in range(2):
                        link(dve.tensor_tensor(by_expert(tmp), by_expert(slots),
                                               slot_f[:, cc, :].unsqueeze(2).to_broadcast([P, NT, NE]), ALU.is_equal))
                        link(dve.tensor_tensor(tmp, tmp, tv, ALU.mult))
                        link(dve.tensor_reduce(wpair[:, cc, :], by_expert(tmp), AX.X, ALU.add))
                    cmp = rt[:, 1024:1024 + NS * NE].rearrange("p (j e) -> p j e", e=NE)
                    link(dve.tensor_tensor(cmp, rc[:, RC_TILE:RC_TILE + NS].unsqueeze(2).to_broadcast([P, NS, NE]),
                                           end.unsqueeze(1).to_broadcast([P, NS, NE]), ALU.is_ge))
                    ef = rt[:, 1500:1500 + NS]
                    link(dve.tensor_reduce(ef, cmp, AX.X, ALU.add))
                    link(dve.tensor_scalar(ef, ef, float(NE - 1), None, ALU.min))
                    dve.tensor_copy(tile_expert, ef)
                    dve.tensor_copy(slot_i, slot_f)
                    dve.tensor_copy(token_i, rc[:, RC_TOKEN:RC_TOKEN + NT]).then_inc(s_rdy, 1)

            (s_ga0, s_ga1, s_ewg0, s_ewg1, s_ewd0, s_ewd1, s_ext, s_exe, s_eg, s_esg, s_et1, s_eh, s_etr, s_etc, s_ey, s_eye, s_eys0, s_eys1,
             s_cga, s_cgb, s_cm) = (
                lsem(n) for n in ("rows_gathered0", "rows_gathered1", "gate_up_load0", "gate_up_load1", "down_load0", "down_load1", "rows_turned2",
                                  "rows_turned_evac", "gate_up_done", "gate_sigmoid", "gate_times", "act_done",
                                  "act_turned", "act_turned_evac", "down_done", "down_evac", "y_stored0", "y_stored1",
                                  "pair_gather0", "pair_gather1", "combine_vec"))
            s_ga, s_ewg, s_ewd, s_eys, s_cg = [s_ga0, s_ga1], [s_ewg0, s_ewg1], [s_ewd0, s_ewd1], [s_eys0, s_eys1], [s_cga, s_cgb]
            LAST = NS - 1
            assert NS % 2 == 1

            def over_tiles(eng, step, first, last):
                j = first
                while j % 2 == 0 or j < 3:
                    step(j, j % 2, j)
                    j += 1
                pairs = (last - j + 1) // 2
                with eng.Fori(0, pairs) as it:
                    step(it * 2 + j, 1, j)
                    step(it * 2 + (j + 1), 0, j)
                for j in range(j + 2 * pairs, last + 1):
                    step(j, j % 2, j)

            with nc.Block() as block:
                @block.sync
                def _(sp):
                    def load_down(j, par, least):
                        e = sp.value_load(tile_expert[0:1, bass.ds(j, 1)], min_val=0, max_val=NE - 1)
                        if least >= 2:
                            sp.wait_ge(s_ey, j - 1)
                        sp.dma_start(exps[:, par, 4096:6144].rearrange("p (k n) -> p k n", k=2),
                                     w_down[layer, e].rearrange("(k p) n -> p k n", p=P)).then_inc(s_ewd[par], 16)

                    def step(j, par, least):
                        e = sp.value_load(tile_expert[0:1, bass.ds(j, 1)], min_val=0, max_val=NE - 1)
                        if least >= 2:
                            sp.wait_ge(s_eg, j - 1)
                        sp.dma_start(exps[:, par, 0:4096].rearrange("p (k n) -> p k n", k=KC),
                                     w_gate_up[layer, e].rearrange("(k p) n -> p k n", p=P)).then_inc(s_ewg[par], 16)
                        if least >= 1:
                            load_down(j - 1, 1 - par, least - 1)
                    over_tiles(sp, step, 0, LAST)
                    load_down(LAST, 0, LAST)

                @block.gpsimd
                def _(pool):
                    for j in range(NS):
                        if j >= 2:
                            pool.wait_ge(s_ext, j - 1)
                        pool.indirect_dma_start(out=hg[:, j % 2, :], out_offset=None, in_=h_dram,
                                                in_offset=bass.IndirectOffsetOnAxis(slot_token[:, j:j + 1], 0))\
                            .then_inc(s_ga[j % 2], 16)
                    pool.wait_ge(s_ga[0], 16 * ((NS + 1) // 2))
                    pool.wait_ge(s_ga[1], 16 * (NS // 2))
                    pool.wait_ge(s_eys[0], 16 * ((NS + 1) // 2))
                    pool.wait_ge(s_eys[1], 16 * (NS // 2))
                    for t in range(NT):
                        if t >= 2:
                            pool.wait_ge(s_cm, 4 * (t - 1))
                        for cc in range(2):
                            pool.indirect_dma_start(out=yab[:, t % 2, cc, :], out_offset=None, in_=y_dram,
                                                    in_offset=bass.IndirectOffsetOnAxis(slot_i[:, cc, t:t + 1], 0))\
                                .then_inc(s_cg[t % 2], 16)
                    pool.wait_ge(s_cg[0], 32 * ((NT + 1) // 2))
                    pool.wait_ge(s_cg[1], 32 * (NT // 2))

                @block.tensor
                def _(pe):
                    def rows(j, par, least):
                        pe.wait_ge(s_ga[par], (j - par) * 8 + 16)
                        if least >= 1:
                            pe.wait_ge(s_exe, j)
                        for k in range(KC):
                            last = pe.transpose(PS[:, k // 4, col(k % 4)], hg[:, par, col(k)], ident)
                        last.then_inc(s_ext, 1)

                    def gate_up(j, par, least):
                        pe.wait_ge(s_exe, j + 1)
                        pe.wait_ge(s_ewg[par], (j - par) * 8 + 16)
                        if least >= 2:
                            pe.wait_ge(s_eh, j - 1)
                        w = exps[:, par, 0:4096].rearrange("p (k n) -> p k n", k=KC)
                        for k in range(KC):
                            last = pe.matmul(PS[:, 2 + par, :], hgT[:, par, k, :], w[:, k, :],
                                             start=(k == 0), stop=(k == KC - 1))
                        last.then_inc(s_eg, 1)

                    def turn(j, par, least):
                        pe.wait_ge(s_eh, j + 1)
                        for f in range(2):
                            last = pe.transpose(PS[:, 4 + par, col(f)], ha[:, par, col(f)], ident)
                        last.then_inc(s_etr, 1)

                    def down(j, par, least):
                        pe.wait_ge(s_etc, j + 1)
                        pe.wait_ge(s_ewd[par], (j - par) * 8 + 16)
                        if least >= 1:
                            pe.wait_ge(s_eye, j)
                        w = exps[:, par, 4096:6144].rearrange("p (k n) -> p k n", k=2)
                        for b in range(2):
                            for f in range(2):
                                last = pe.matmul(PS[:, 6 + b, :], haT[:, par, col(f)], w[:, f, col(b, 512)],
                                                 start=(f == 0), stop=(f == 1))
                        last.then_inc(s_ey, 1)

                    def step(j, par, least):
                        gate_up(j, par, least)
                        if least >= 1:
                            turn(j - 1, 1 - par, least - 1)
                        if not isinstance(j, int) or j < LAST:
                            rows(j + 1, 1 - par, least + 1)
                        if least >= 1:
                            down(j - 1, 1 - par, least - 1)
                    rows(0, 0, 0)
                    over_tiles(pe, step, 0, LAST - 2)
                    step(LAST - 1, 1, LAST - 1)
                    step(LAST, 0, LAST)
                    turn(LAST, 0, LAST)
                    down(LAST, 0, LAST)

                @block.scalar
                def _(act):
                    def rows_evac(j, par, least):
                        act.wait_ge(s_ext, j + 1)
                        if least >= 2:
                            act.wait_ge(s_eg, j - 1)
                        act.activation(hgT[:, par, :, :].rearrange("p k n -> p (k n)"),
                                       PS[:, 0:2, :].rearrange("p b n -> p (b n)"), ACT.Copy).then_inc(s_exe, 1)

                    def store(j, par):
                        act.wait_ge(s_eye, j + 1)
                        act.dma_start(y_dram[bass.ds(j * P, P), :], ys[:, par, :]).then_inc(s_eys[par], 16)

                    def step(j, par, least):
                        act.wait_ge(s_eg, j + 1)
                        if least >= 2:
                            act.wait_ge(s_eh, j - 1)
                        act.activation(sg[:, par, :], PS[:, 2 + par, 0:DE], ACT.Sigmoid).then_inc(s_esg, 1)
                        if least >= 1:
                            act.wait_ge(s_etr, j)
                            if least >= 3:
                                act.wait_ge(s_ey, j - 2)
                            act.activation(haT[:, 1 - par, :], PS[:, 5 - par, 0:DE], ACT.Copy).then_inc(s_etc, 1)
                        if not isinstance(j, int) or j < LAST:
                            rows_evac(j + 1, 1 - par, least + 1)
                        if least >= 2:
                            store(j - 2, par)
                    rows_evac(0, 0, 0)
                    over_tiles(act, step, 0, LAST - 2)
                    step(LAST - 1, 1, LAST - 1)
                    step(LAST, 0, LAST)
                    act.wait_ge(s_etr, LAST + 1)
                    act.activation(haT[:, 0, :], PS[:, 4, 0:DE], ACT.Copy).then_inc(s_etc, 1)
                    store(LAST - 1, 1)
                    store(LAST, 0)
                    act.wait_ge(s_eys[0], 16 * ((NS + 1) // 2))
                    act.wait_ge(s_eys[1], 16 * (NS // 2))

                @block.vector
                def _(dve):
                    def out(j, par, least):
                        dve.wait_ge(s_ey, j + 1)
                        if least >= 2:
                            dve.wait_ge(s_eys[par], (j - par) * 8)
                        dve.tensor_copy(ys[:, par, :], PS[:, 6:8, :].rearrange("p b n -> p (b n)")).then_inc(s_eye, 1)

                    def step(j, par, least):
                        dve.wait_ge(s_esg, j + 1)
                        dve.tensor_tensor(sg[:, par, :], PS[:, 2 + par, 0:DE], sg[:, par, :], ALU.mult)\
                           .then_inc(s_et1, 1)
                        dve.wait_ge(s_et1, j + 1)
                        if least >= 2:
                            dve.wait_ge(s_etr, j - 1)
                        dve.tensor_tensor(ha[:, par, :], sg[:, par, :], PS[:, 2 + par, DE:2 * DE], ALU.mult)\
                           .then_inc(s_eh, 1)
                        if least >= 1:
                            out(j - 1, 1 - par, least - 1)
                    over_tiles(dve, step, 0, LAST)
                    out(LAST, 0, LAST)
                    for t in range(NT):
                        ya, yb = yab[:, t % 2, 0, :], yab[:, t % 2, 1, :]
                        dve.wait_ge(s_cg[t % 2], 32 * (t // 2 + 1))
                        dve.tensor_scalar(ya, ya, wpair[:, 0, t:t + 1], None, ALU.mult).then_inc(s_cm, 1)
                        dve.wait_ge(s_cm, 4 * t + 1)
                        dve.scalar_tensor_tensor(ya, yb, wpair[:, 1, t:t + 1], ya, ALU.mult, ALU.add).then_inc(s_cm, 1)
                        dve.wait_ge(s_cm, 4 * t + 2)
                        dve.tensor_tensor(ya, ya, g2b[:, 1 if t else 0, :], ALU.mult).then_inc(s_cm, 1)
                        dve.wait_ge(s_cm, 4 * t + 3)
                        dve.tensor_tensor(x[:, t, :], x[:, t, :], ya, ALU.add).then_inc(s_cm, 1)

            with nc.Block() as block:
                @block.gpsimd
                def _(pool):
                    pool.dma_reset(range(layer_sems[0].num, layer_sems[-1].num + 1))
                    for s in layer_sems:
                        pool.sem_clear(s)
            lay_ctx.close()

        with ExitStack() as fin_ctx:
            s_fl, s_fs, s_fm, s_fp, s_fx, s_fv, s_fo = (
                fin_ctx.enter_context(nc.semaphore(n)) for n in
                ("final_load", "final_sq", "final_mean", "final_rstd", "final_scaled", "final_vec", "final_stored"))
            fg = T[:, 0:D]
            yo = T[:, D:D + NT * D].rearrange("p (t n) -> p t n", t=NT)
            ss, ms, rs = small[:, 64:64 + NT], small[:, 72:72 + NT], small[:, 80:80 + NT]
            with nc.Block() as block:
                @block.sync
                def _(sp):
                    sp.dma_start(fg, final_g.partition_broadcast(P)).then_inc(s_fl, 16)
                    for t in range(NT):
                        sp.wait_ge(s_fv, t + 1)
                        dst = y_prompt[0] if t == 0 else y_sample[0, (t - 1) * P:t * P, :]
                        sp.dma_start(dst, yo[:, t, :]).then_inc(s_fo, 16)
                    sp.wait_ge(s_fo, NT * 16)

                @block.scalar
                def _(act):
                    for t in range(NT):
                        act.activation(yo[:, t, :], x[:, t, :], ACT.Square, accum_out=ss[:, t:t + 1]).then_inc(s_fs, 1)
                    act.wait_ge(s_fp, 1)
                    act.wait_ge(s_fs, NT)
                    for t in range(NT):
                        act.activation(yo[:, t, :], x[:, t, :], ACT.Copy, scale=rs[:, t:t + 1]).then_inc(s_fx, 1)

                @block.gpsimd
                def _(pool):
                    pool.wait_ge(s_fm, 1)
                    pool.tensor_tensor(rs, ms, minus_half[:, 0:NT], ALU.pow).then_inc(s_fp, 1)

                @block.vector
                def _(dve):
                    dve.wait_ge(s_fs, NT)
                    dve.tensor_scalar(ms, ss, 1.0 / D, EPS, ALU.mult, ALU.add).then_inc(s_fm, 1)
                    dve.wait_ge(s_fl, 16)
                    for t in range(NT):
                        dve.wait_ge(s_fx, t + 1)
                        dve.tensor_tensor(yo[:, t, :], yo[:, t, :], fg, ALU.mult).then_inc(s_fv, 1)


def constants():
    import numpy as np
    cst = np.zeros((P, C_END), np.float32)
    cst[:, C_IDENT:C_IDENT + P] = np.eye(P)
    p, j = np.arange(P)[:, None], np.arange(P)[None, :]
    cst[:, C_WIN:C_WIN + P] = np.where(j >= p, 0.0, -1e30)
    cst[:, C_WIN + 3 * P:C_WIN + 4 * P] = np.where(j <= p, 0.0, -1e30)
    n_freq = HD // 4
    freqs = (np.float32(10000.0) ** (-np.arange(n_freq, dtype=np.float32) / np.float32(n_freq))).astype(np.float32)
    tok = np.arange(NL * P)
    pos = np.stack([tok // 64, tok % 64], 1).astype(np.float32)
    angle = (pos[:, :, None] * freqs).astype(np.float32).reshape(NL, P, 2 * n_freq)
    pair = np.concatenate([angle, angle], 2)
    cst[:, C_COS:C_COS + 2 * P] = np.cos(pair).transpose(1, 0, 2).reshape(P, 2 * P)
    cst[:, C_SIN:C_SIN + 2 * P] = np.sin(pair).transpose(1, 0, 2).reshape(P, 2 * P)
    i4, j4 = np.arange(4)[:, None], np.arange(4)[None, :]
    cst[:, C_LT:C_LT + 16] = (j4 < i4).astype(np.float32).reshape(1, 16)
    masks = np.zeros((P, 2, len(LEVELS) + 1, P), np.float32)
    s, t = p, j
    masks[:, :, 0] = (s == t)[:, None, :]
    for lv, h in enumerate(LEVELS, start=1):
        same = (s // (2 * h)) == (t // (2 * h))
        low, high = (s // h) % 2 == 0, (t // h) % 2 == 1
        masks[:, 0, lv] = same & low & high
        masks[:, 1, lv] = same & ~low & ~high
    route = np.zeros((P, RC_END), np.float32)
    route[:, RC_BEFORE:RC_BEFORE + P] = p < j
    route[:, RC_ONES:RC_ONES + P] = 1.0
    route[:, RC_TILE:RC_TILE + NS] = np.arange(NS)
    route[:, RC_TOKEN:RC_TOKEN + NT] = p + P * np.arange(NT)
    return cst, masks.reshape(P, -1), route


_INS = ["x_prompt", "x_sample", "cache_glob_k", "cache_glob_v", "cache_win_k", "cache_win_v", "state_hgrn", "c",
        "c_ctx", "mod_w", "mod_b", "norm1_g", "norm2_g", "w_in", "w_out", "hgrn_lb", "hgrn_norm_g", "q_norm_g",
        "k_norm_g", "win_sink", "router_w", "router_b", "w_gate_up", "w_down", "final_g"]
_OUTS = [(1, P, D), (1, NL * P, D)] + [(1, DEPTH, P, KVH, HD)] * 4 + [(1, DEPTH, 2, AH, HD, HD)]


def kernel(**inputs):
    import numpy as np
    import concourse.bacc as bacc
    from concourse.bass_utils import run_bass_kernel_spmd

    nc = bacc.Bacc("TRN2", target_bir_lowering=False, num_devices=1)
    arrays, args = {}, []
    cst, masks, route = constants()
    for name, a in [(n, inputs[n]) for n in _INS] + [("consts", cst), ("masks", masks), ("route", route)]:
        a = np.ascontiguousarray(a)
        arrays[f"in_{name}"] = a
        args.append(nc.dram_tensor(f"in_{name}", a.shape, mybir.dt.from_np(a.dtype), kind="ExternalInput").ap())
    for i, shape in enumerate(_OUTS):
        args.append(nc.dram_tensor(f"out_{i}", shape, F32, kind="ExternalOutput").ap())
    program(nc, *args)
    r = run_bass_kernel_spmd(nc, [arrays], core_ids=[0])
    return tuple(r.results[0][f"out_{i}"] for i in range(len(_OUTS)))
```

```python
from contextlib import ExitStack

import concourse.bass as bass
from concourse import mybir

F32 = mybir.dt.float32
I32 = mybir.dt.int32
U8 = mybir.dt.uint8
ALU = mybir.AluOpType
ACT = mybir.ActivationFunctionType
AX = mybir.AxisListType

P = 128
D = 1024
KC = D // P
DEPTH = 2
NL = 4
NT = NL + 1
TOK = NT * P
HD = 64
AH = 4
AW = AH * HD
QH = 6
KVH = 2
G = QH // KVH
QW = QH * HD
KVW = KVH * HD
INW = 5 * AW + 2 * (QW + 2 * KVW)
NE = 16
EPG = 4
NG = NE // EPG
DE = 256
EPS = 1e-6
TINY = 1e-30
SCALE = HD ** -0.5
LEVELS = [1, 2, 4, 8, 16, 32, 64]
KEYS = TOK + P
MODC = 6 * KC
C_IDENT, C_WIN, C_COS, C_SIN, C_LT = 0, 128, 640, 896, 1152
C_END = C_LT + 16


T_SIZE = 19456
NS = (2 * TOK + NE * (P - 1)) // P
RC_BEFORE, RC_ONES, RC_TILE, RC_TOKEN = 0, P, 2 * P, 2 * P + NS
RC_IOTA = RC_TOKEN + NT
RC_END = RC_IOTA + P


def col(t, n=P):
    return slice(t * n, (t + 1) * n)


def program(nc, x_prompt, x_sample, cgk, cgv, cwk, cwv, state, c, c_ctx, mod_w, mod_b, norm1_g, norm2_g,
            w_in, w_out, hgrn_lb, hgrn_norm_g, q_norm_g, k_norm_g, win_sink, router_w, router_b,
            w_gate_up, w_down, final_g, consts, masks, route_consts,
            y_prompt, y_sample, new_gk, new_gv, new_wk, new_wv, new_state):
    ctx = ExitStack()
    with ctx:
        def sb(name, shape, dt=F32):
            return ctx.enter_context(nc.sbuf_tensor(name, shape, dt))

        def sem(name):
            return ctx.enter_context(nc.semaphore(name))

        cst = sb("cst", [P, C_END])
        ident = cst[:, C_IDENT:C_IDENT + P]
        winmask = cst[:, C_WIN:C_WIN + 512]
        cosT = cst[:, C_COS:C_COS + 2 * P].rearrange("p (t m f) -> p t m f", t=NL, m=4)
        sinT = cst[:, C_SIN:C_SIN + 2 * P].rearrange("p (t m f) -> p t m f", t=NL, m=4)
        ltmask = cst[:, C_LT:C_LT + 16]
        levelmask = sb("levelmask", [P, 2, len(LEVELS) + 1, P], U8)
        x = sb("x", [P, NT, D])
        hT = sb("hT", [P, KC, TOK])
        W = sb("W", [P, KC * INW])
        condT = sb("condT", [P, KC, 2])
        lball = sb("lball", [P, DEPTH, 2, 2])
        lb = sb("lb", [P, 2, 2])
        olb = sb("olb", [P, 2, 2])
        modc = sb("modc", [P, MODC, 2])
        scale1 = sb("scale1", [P, KC, 2])
        scale2 = sb("scale2", [P, KC, 2])
        small = sb("small", [P, 512])
        minus_half = sb("minus_half", [P, 64])
        qkg = sb("qkg", [P, 2, HD])
        ang = sb("ang", [P, HD])
        sink = sb("sink", [P, QH])
        rbias = sb("rbias", [P, NE])
        T = sb("T", [P, T_SIZE])
        PS = ctx.enter_context(nc.psum_tensor("PS", [P, 8, 512], F32))

        top = [0]

        def carve(n, **shape):
            a = T[:, top[0]:top[0] + n]
            top[0] += n
            return a

        va = carve(NT * AW).rearrange("p (t n) -> p t n", t=NT)
        ga = carve(NT * AW).rearrange("p (t n) -> p t n", t=NT)
        vg = carve((NT + 1) * KVW).rearrange("p (t n) -> p t n", t=NT + 1)
        vw = carve((NT + 1) * KVW).rearrange("p (t n) -> p t n", t=NT + 1)
        qT = carve(2 * G * TOK).rearrange("p (w j n) -> p w j n", w=2, j=G)
        kT = carve(2 * KEYS).rearrange("p (w n) -> p w n", w=2)
        QQ = carve(2 * TOK).rearrange("p (f n) -> p f n", f=2)
        QF = carve(4 * TOK).rearrange("p (d f n) -> p d f n", d=2, f=2)
        KK = carve(4 * TOK).rearrange("p (d f n) -> p d f n", d=2, f=2)
        tail = top[0]
        zs = carve(2 * 1792).rearrange("p (s n) -> p s n", s=2)
        xn = zs.rearrange("p s n -> p (s n)")[:, 0:2 * D].rearrange("p (s n) -> p s n", s=2)
        assert top[0] <= T_SIZE, top[0]
        modw = T[:, 0:2 * KC * 512].rearrange("p (s k n) -> p s k n", s=2, k=KC)
        modrow = T[:, 2 * KC * 512 + 3 * P:2 * KC * 512 + 3 * P + 1024].rearrange("p (s n) -> p s n", s=2)
        rows = T[:, 2 * KC * 512:2 * KC * 512 + 3 * P].rearrange("p (s n) -> p s n", s=3)
        win = W[:, :].rearrange("p (k n) -> p k n", k=KC)
        wout = W[:, 0:KC * D].rearrange("p (k n) -> p k n", k=KC)
        exps = W[:, KC * D:KC * D + 2 * 6144].rearrange("p (s n) -> p s n", s=2)
        M = W[:, KC * D:KC * D + 4 * TOK].rearrange("p (d f n) -> p d f n", d=2, f=2)
        KF = W[:, KC * D + 4 * TOK:KC * D + 8 * TOK].rearrange("p (d f n) -> p d f n", d=2, f=2)
        Am = hT[:, :, :].rearrange("p k n -> p (k n)").rearrange("p (d t a n) -> p d t a n", d=2, t=NT, a=AH)
        sv0 = KC * D + 8 * TOK
        Sv = W[:, sv0:sv0 + 2048].rearrange("p (d s f n) -> p d s f n", d=2, s=4, f=2)
        modw2 = W[:, 0:2 * KC * 512].rearrange("p (s k n) -> p s k n", s=2, k=KC)
        oall = W[:, KC * INW - NT * D:].rearrange("p (t n) -> p t n", t=NT)
        assert sv0 + 2048 <= KC * INW - NT * D
        modrow2 = oall[:, 0:2, 0:AW]
        GK, WK = NT * P, 4 * P
        tt = [tail]

        def carve1(n):
            a = T[:, tt[0]:tt[0] + n]
            tt[0] += n
            return a

        pr = [carve1(GK), carve1(WK)]
        prT = [carve1(GK), carve1(WK)]
        sm = carve1(WK)
        kout = carve1(AW)
        Sc = carve1(256).rearrange("p (d f n) -> p d f n", d=2, f=2)
        assert tt[0] <= T_SIZE
        osum = KF.rearrange("p d f n -> p (d f n)")[:, 0:NT * AW].rearrange("p (t n) -> p t n", t=NT)
        osq = KF.rearrange("p d f n -> p (d f n)")[:, NT * AW:2 * NT * AW].rearrange("p (t n) -> p t n", t=NT)
        g1b = T[:, tail:tail + 2 * D].rearrange("p (s n) -> p s n", s=2)
        oT = T[:, 0:2 * KC * P].rearrange("p (s k n) -> p s k n", s=2, k=KC)
        prod = T[:, 2048:2048 + 2 * D].rearrange("p (s n) -> p s n", s=2)
        tt[0] = 0

        def carve2(n):
            a = T[:, tt[0]:tt[0] + n]
            tt[0] += n
            return a

        g2b = carve2(2 * D).rearrange("p (s n) -> p s n", s=2)
        rw = carve2(KC * NE).rearrange("p (k n) -> p k n", k=KC)
        rc = carve2(RC_END)
        slot_f = carve2(2 * NT).rearrange("p (c t) -> p c t", c=2)
        wpair = carve2(2 * NT).rearrange("p (c t) -> p c t", c=2)
        slot_i = carve2(2 * NT).bitcast(I32).rearrange("p (c t) -> p c t", c=2)
        slot_token = carve2(NS + 1).bitcast(I32)
        tile_expert = carve2(NS).bitcast(I32)
        tile_used = carve2(NS).bitcast(I32)
        tiles_looped = carve2(1).bitcast(I32)
        e0 = tt[0]
        arow = carve2(2 * D).rearrange("p (s n) -> p s n", s=2)
        brow = carve2(2 * D).rearrange("p (s n) -> p s n", s=2)
        h2 = carve2(NT * D).rearrange("p (t n) -> p t n", t=NT)
        rt = carve2(4096)
        assert tt[0] <= T_SIZE
        tt[0] = e0
        hg = carve2(2 * D).rearrange("p (s n) -> p s n", s=2)
        hgT = carve2(2 * D).rearrange("p (s k n) -> p s k n", s=2, k=KC)
        ys = carve2(2 * D).rearrange("p (s n) -> p s n", s=2)
        sg, ha, haT = (carve2(2 * DE).rearrange("p (s n) -> p s n", s=2) for _ in range(3))
        yab = carve2(4 * D).rearrange("p (s c n) -> p s c n", s=2, c=2)
        assert tt[0] <= T_SIZE
        h_dram = nc.dram_tensor("h_rows", (TOK, D), F32, kind="Internal").ap()
        y_dram = nc.dram_tensor("y_rows", (NS * P, D), F32, kind="Internal").ap()

        def chain(eng, s, start=0):
            count = [start]

            def link(ins):
                count[0] += 1
                ins.then_inc(s, 1)
                eng.wait_ge(s, count[0])
            return link

        with ExitStack() as st:
            def ssem(name):
                return st.enter_context(nc.semaphore(name))
            s_ld, s_pe, s_v, s_a, s_g = (ssem(n) for n in ("set_load", "set_pe", "set_vec", "set_act", "set_pool"))
            crow = T[0:8, 0:3 * P].rearrange("p (s n) -> p s n", s=3)
            mask_f32 = T[:, 1024:1024 + 2 * (len(LEVELS) + 1) * P]
            lbc = small[:, 0:8].rearrange("p (d l f) -> p d l f", d=2, l=DEPTH)
            block = st.enter_context(nc.Block())

            @block.sync
            def _(sp):
                sp.dma_start(cst[:, :], consts).then_inc(s_ld, 16)
                sp.dma_start(mask_f32, masks).then_inc(s_ld, 16)
                sp.dma_start(crow[:, 0, :], c_ctx.rearrange("(a b) -> a b", b=P)).then_inc(s_ld, 16)
                sp.dma_start(crow[:, 1, :], c.rearrange("o (a b) -> (o a) b", b=P)).then_inc(s_ld, 16)
                sp.dma_start(crow[:, 2, :], hgrn_lb.rearrange("d l (f b) -> (d l f) b", b=P)).then_inc(s_ld, 16)
                sp.dma_start(x[:, 0, :], x_prompt[0]).then_inc(s_ld, 16)
                sp.dma_start(x[:, 1:NT, :], x_sample[0].rearrange("(t p) n -> p t n", p=P)).then_inc(s_ld, 16)
                sp.dma_start(rbias[:, :], router_b.partition_broadcast(P)).then_inc(s_ld, 16)
                sp.wait_ge(s_ld, 8 * 16)

            @block.gpsimd
            def _(pool):
                pool.memset(minus_half[:, :], -0.5).then_inc(s_g, 1)
                pool.wait_ge(s_g, 1)

            @block.tensor
            def _(pe):
                pe.wait_ge(s_ld, 8 * 16)
                for s in range(3):
                    last = pe.transpose(PS[:, 0, s * 8:s * 8 + 8], crow[:, s, :], ident[0:8, 0:8])
                last.then_inc(s_pe, 1)

            @block.scalar
            def _(act):
                act.wait_ge(s_v, 1)
                act.activation(small[:, 16:32], PS[:, 0, 0:16], ACT.Sigmoid).then_inc(s_a, 1)
                act.wait_ge(s_v, 3)
                act.activation(small[:, 48:56], small[:, 40:48], ACT.Exp).then_inc(s_a, 1)

            @block.vector
            def _(dve):
                link = chain(dve, s_v)
                dve.wait_ge(s_pe, 1)
                link(dve.tensor_copy(small[:, 0:8], PS[:, 0, 16:24]))
                dve.tensor_copy(levelmask[:, :, :, :].rearrange("p a b c -> p (a b c)"), mask_f32)
                mx = small[:, 56:60].rearrange("p (d f) -> p d f", d=2)
                link(dve.tensor_tensor(mx, lbc[:, :, 0, :], lbc[:, :, 1, :], ALU.max))
                ex = small[:, 40:48].rearrange("p (d l f) -> p d l f", d=2, l=DEPTH)
                link(dve.tensor_tensor(ex, lbc, mx.unsqueeze(2).to_broadcast([P, 2, DEPTH, 2]), ALU.subtract))
                dve.wait_ge(s_a, 1)
                link(dve.tensor_tensor(condT[:, :, :].rearrange("p k s -> p s k"),
                                       PS[:, 0, 0:16].rearrange("p (s k) -> p s k", s=2),
                                       small[:, 16:32].rearrange("p (s k) -> p s k", s=2), ALU.mult))
                dve.wait_ge(s_a, 2)
                e = small[:, 48:56].rearrange("p (d l f) -> p d l f", d=2, l=DEPTH)
                link(dve.tensor_tensor(mx, e[:, :, 0, :], e[:, :, 1, :], ALU.add))
                link(dve.reciprocal(mx, mx))
                link(dve.tensor_tensor(e, e, mx.unsqueeze(2).to_broadcast([P, 2, DEPTH, 2]), ALU.mult))
                link(dve.tensor_tensor(lball[:, 0, :, :], e[:, :, 0, :], e[:, :, 0, :], ALU.subtract))
                link(dve.tensor_tensor(lball[:, 1, :, :], e[:, :, 0, :], e[:, :, 1, :], ALU.add))
                link(dve.tensor_tensor(lball[:, 1, :, :], lball[:, 1, :, :], e[:, :, 0, :], ALU.subtract))

        lay_ctx = ExitStack()
        layer_sems = []

        def lsem(name):
            s = lay_ctx.enter_context(nc.semaphore(name))
            layer_sems.append(s)
            return s

        with nc.Fori(0, DEPTH) as layer:
            s_row, s_mw0, s_mw1, s_mr, s_mre, s_mt, s_rowT, s_mv, s_win, s_par = (
                lsem(n) for n in ("rows_load", "modw_load0", "modw_load1", "mod_rows", "mod_rows_evac", "mod_turned",
                                  "rows_turned", "mod_vec", "win_load", "params_load"))
            s_mw = [s_mw0, s_mw1]
            MOD1 = 4
            s_sq, s_ms, s_pw, s_xn, s_tr, s_ev = (lsem(f"norm1_{n}") for n in
                                                  ("squares", "mean", "rstd", "scaled", "turned", "evac"))
            ss, ms, rs = small[:, 64:64 + NT], small[:, 72:72 + NT], small[:, 80:80 + NT]
            ck = small[:, 128:384].rearrange("p (s n) -> p s n", s=2)

            def load_mod(sp, n, w):
                if n >= 2:
                    sp.wait_ge(s_mr, n - 1)
                sp.dma_start(w[:, n % 2, :, :], mod_w[layer, :, col(n, 512)].rearrange("(k p) n -> p k n", p=P))\
                  .then_inc(s_mw[n % 2], 16)

            def mod_rows(pe, n, w, bank0):
                pe.wait_ge(s_mw[n % 2], 16 * (n // 2 + 1))
                if n >= 2:
                    pe.wait_ge(s_mre, n - 1)
                for k in range(KC):
                    last = pe.matmul(PS[0:2, bank0 + n % 2, :], condT[:, k, :], w[:, n % 2, k, :],
                                     start=(k == 0), stop=(k == KC - 1))
                last.then_inc(s_mr, 1)

            def mod_rows_evac(act, n, dst, bank0):
                act.wait_ge(s_mr, n + 1)
                if n >= 2:
                    act.wait_ge(s_mt, n - 1)
                act.activation(dst[0:2, n % 2, :], PS[0:2, bank0 + n % 2, :], ACT.Copy).then_inc(s_mre, 1)

            def mod_turn(pe, n, src, bank):
                pe.wait_ge(s_mre, n + 1)
                for m in range(4):
                    last = pe.transpose(PS[:, bank, 2 * (4 * n + m):2 * (4 * n + m) + 2], src[0:2, n % 2, col(m)],
                                        ident[0:2, 0:2])
                last.then_inc(s_mt, 1)

            def mod_finish(dve, link, n0, n1, bank, dst, sc0, g0):
                dve.wait_ge(s_mt, n1)
                link(dve.tensor_tensor(modc[:, 4 * n0:4 * n1, :],
                                       PS[:, bank, 8 * n0:8 * n1].rearrange("p (m s) -> p m s", s=2),
                                       small[:, 4 * n0:4 * n1].unsqueeze(2).to_broadcast([P, 4 * (n1 - n0), 2]),
                                       ALU.add))
                link(dve.tensor_scalar(dst[:, :, :], modc[:, sc0:sc0 + KC, :], 1.0, None, ALU.add))
                link(dve.tensor_tensor(dst[:, :, :], dst[:, :, :],
                                       small[:, g0:g0 + KC].unsqueeze(2).to_broadcast([P, KC, 2]), ALU.mult))

            with nc.Block() as block:
                @block.sync
                def _(sp):
                    sp.dma_start(rows[0:48, 0, :], mod_b[layer].rearrange("(a b) -> a b", b=P)).then_inc(s_row, 16)
                    sp.dma_start(rows[0:8, 1, :], norm1_g[layer].rearrange("(a b) -> a b", b=P)).then_inc(s_row, 16)
                    sp.dma_start(rows[0:8, 2, :], norm2_g[layer].rearrange("(a b) -> a b", b=P)).then_inc(s_row, 16)
                    load_mod(sp, 0, modw)
                    load_mod(sp, 1, modw)
                    sp.dma_start(qkg[:, 0, :], q_norm_g[layer].partition_broadcast(P)).then_inc(s_par, 16)
                    sp.dma_start(qkg[:, 1, :], k_norm_g[layer].partition_broadcast(P)).then_inc(s_par, 16)
                    sp.dma_start(ang[:, :], hgrn_norm_g[layer].partition_broadcast(P)).then_inc(s_par, 16)
                    sp.dma_start(sink[:, :], win_sink[layer].partition_broadcast(P)).then_inc(s_par, 16)
                    load_mod(sp, 2, modw)
                    load_mod(sp, 3, modw)
                    for k in range(KC):
                        sp.dma_start(win[:, k, :], w_in[layer, col(k), :]).then_inc(s_win, 16)

                @block.tensor
                def _(pe):
                    pe.wait_ge(s_row, 3 * 16)
                    pe.transpose(PS[:, 3, 0:48], rows[0:48, 0, :], ident[0:48, 0:48])
                    pe.transpose(PS[:, 3, 48:56], rows[0:8, 1, :], ident[0:8, 0:8])
                    pe.transpose(PS[:, 3, 56:64], rows[0:8, 2, :], ident[0:8, 0:8]).then_inc(s_rowT, 1)

                    def turn_tile(t):
                        pe.wait_ge(s_xn, t + 1)
                        if t >= 2:
                            pe.wait_ge(s_ev, t - 1)
                        for k in range(KC):
                            last = pe.transpose(PS[:, 4 + 2 * (t % 2) + k // 4, col(k % 4)], xn[:, t % 2, col(k)], ident)
                        last.then_inc(s_tr, 1)

                    turn_tile(0)
                    turn_tile(1)
                    for n in range(MOD1):
                        mod_rows(pe, n, modw, 0)
                        if n >= 1:
                            mod_turn(pe, n - 1, modrow, 2)
                    mod_turn(pe, MOD1 - 1, modrow, 2)
                    for t in range(2, NT):
                        turn_tile(t)

                @block.gpsimd
                def _(pool):
                    pool.wait_ge(s_ms, 1)
                    pool.tensor_tensor(rs, ms, minus_half[:, 0:NT], ALU.pow).then_inc(s_pw, 1)

                @block.scalar
                def _(act):
                    def scaled(t):
                        if t >= 2:
                            act.wait_ge(s_tr, t - 1)
                        act.activation(xn[:, t % 2, :], x[:, t, :], ACT.Copy, scale=rs[:, t:t + 1]).then_inc(s_xn, 1)

                    for t in range(NT):
                        if t >= 1:
                            act.wait_ge(s_sq, t)
                        act.activation(xn[:, 0, :], x[:, t, :], ACT.Square,
                                       accum_out=ss[:, t:t + 1]).then_inc(s_sq, 1)
                    act.wait_ge(s_pw, 1)
                    act.wait_ge(s_sq, NT)
                    scaled(0)
                    scaled(1)
                    for n in range(MOD1):
                        mod_rows_evac(act, n, modrow, 0)
                    for t in range(2, NT):
                        scaled(t)

                @block.vector
                def _(dve):
                    link = chain(dve, s_mv)
                    dve.wait_ge(s_sq, NT)
                    dve.tensor_scalar(ms, ss, 1.0 / D, EPS, ALU.mult, ALU.add).then_inc(s_ms, 1)
                    dve.wait_ge(s_rowT, 1)
                    link(dve.tensor_copy(small[:, 0:64], PS[:, 3, 0:64]))
                    link(dve.tensor_copy(lb[:, :, :], lball[:, bass.ds(layer, 1), :, :].rearrange("p o d f -> p (o d) f")))
                    link(dve.tensor_scalar(olb[:, :, :], lb[:, :, :], -1.0, 1.0, ALU.mult, ALU.add))
                    mod_finish(dve, link, 0, MOD1, 2, scale1, KC, 48)
                    for t in range(NT):
                        dve.wait_ge(s_tr, t + 1)
                        cond = 1 if t else 0
                        for k in range(KC):
                            last = dve.tensor_scalar(hT[:, k, col(t)], PS[:, 4 + 2 * (t % 2) + k // 4, col(k % 4)],
                                                     scale1[:, k, cond:cond + 1], modc[:, k, cond:cond + 1],
                                                     ALU.mult, ALU.add)
                        last.then_inc(s_ev, 1)

            o_qa, o_ia, o_fa, o_fb, o_ga = 0, AW, 2 * AW, 3 * AW, 4 * AW
            o_qg = 5 * AW
            o_kg, o_vg = o_qg + QW, o_qg + QW + KVW
            o_qw = o_vg + KVW
            o_kw, o_vw = o_qw + QW, o_qw + QW + KVW
            NGRP = 7
            s_z, s_ze, s_zc, s_rd, s_rp, s_rot, s_tp, s_te, s_qs, s_qm, s_cl, s_ct, s_cte, s_co = (
                lsem(n) for n in ("z_done", "z_evac", "qk_vec", "qk_mean", "qk_rstd", "rotated", "z_turned",
                                  "turned_evac_act", "q_sigmoid", "turned_evac_vec", "cache_loaded", "cache_turned",
                                  "cache_evac", "ctx_stored"))
            SG, SW = 768, 1280
            with nc.Block() as block:
                @block.sync
                def _(sp):
                    sp.dma_start(ck[:, 0, :], cgk[0, layer].rearrange("s h d -> s (h d)")).then_inc(s_cl, 16)
                    sp.dma_start(ck[:, 1, :], cwk[0, layer].rearrange("s h d -> s (h d)")).then_inc(s_cl, 16)
                    sp.dma_start(vg[:, NT, :], cgv[0, layer].rearrange("s h d -> s (h d)")).then_inc(s_cl, 16)
                    sp.dma_start(vw[:, NT, :], cwv[0, layer].rearrange("s h d -> s (h d)")).then_inc(s_cl, 16)
                    sp.wait_ge(s_ze, NGRP)
                    sp.dma_start(new_gv[0, layer].rearrange("s h d -> s (h d)"), vg[:, 0, :]).then_inc(s_co, 16)
                    sp.dma_start(new_wv[0, layer].rearrange("s h d -> s (h d)"), vw[:, 0, :]).then_inc(s_co, 16)
                    sp.dma_start(new_wk[0, layer].rearrange("s h d -> s (h d)"),
                                 zs[:, 0, SW + QW:SW + QW + KVW]).then_inc(s_co, 16)
                    sp.wait_ge(s_rot, 1)
                    sp.dma_start(new_gk[0, layer].rearrange("s h d -> s (h d)"),
                                 hT[:, 3, col(0)]).then_inc(s_co, 16)
                    sp.wait_ge(s_co, 4 * 16)

                @block.tensor
                def _(pe):
                    pe.wait_ge(s_cl, 4 * 16)
                    pe.transpose(PS[:, 4, 0:P], ck[:, 0, :], ident)
                    pe.transpose(PS[:, 4, P:2 * P], ck[:, 1, :], ident).then_inc(s_ct, 1)
                    pe.wait_ge(s_win, KC * 16)

                    def turn(t):
                        pe.wait_ge(s_rot, t + 1)
                        pe.wait_ge(s_te, t + 1)
                        if t >= 1:
                            pe.wait_ge(s_qm, 2 * t)
                        for s in range(2):
                            for j in range(4):
                                pe.transpose(PS[:, 4 + s, col(j)], hT[:, 4 * s + j, col(t)], ident)
                        for j in range(6):
                            last = pe.transpose(PS[:, 6 + j // 4, col(j % 4)], zs[:, t % 2, col(j)], ident)
                        last.then_inc(s_tp, 1)

                    grp = 0
                    for t in range(NT):
                        for n in range(NGRP):
                            if grp >= 4:
                                pe.wait_ge(s_ze, grp - 3)
                            for k in range(KC):
                                lhsT = hT[:, k, col(t)]
                                if n in (0, 2):
                                    o = o_qg if n == 0 else o_qw
                                    rhs = win[:, k, o:o + QW].rearrange("p (v j d) -> p j v d", v=KVH, j=G)
                                    out = PS[:, grp % 4, 0:QW].rearrange("p (j v d) -> p j v d", v=KVH, j=G)
                                else:
                                    o, w = {1: (o_kg, 256), 3: (o_kw, 256), 4: (o_fa, 512), 5: (o_qa, 512),
                                            6: (o_ga, 256)}[n]
                                    rhs, out = win[:, k, o:o + w], PS[:, grp % 4, 0:w]
                                last = pe.matmul(out, lhsT, rhs, start=(k == 0), stop=(k == KC - 1))
                            last.then_inc(s_z, 1)
                            grp += 1
                        if t >= 1:
                            turn(t - 1)
                    turn(NT - 1)

                @block.scalar
                def _(act):
                    def turned(t):
                        act.wait_ge(s_tp, t + 1)
                        gates = PS[:, 6, :].rearrange("p (g n) -> p g n", g=4)
                        act.activation(QQ[:, :, col(t)], PS[:, 7, 0:2 * P].rearrange("p (f n) -> p f n", f=2),
                                       ACT.Sigmoid).then_inc(s_qs, 1)
                        act.activation(QF[:, :, :, col(t)].rearrange("p d f n -> p (d f) n"), gates, ACT.Sigmoid)
                        act.activation(KK[:, :, :, col(t)].rearrange("p d f n -> p (d f) n"), gates, ACT.Sigmoid,
                                       scale=-1.0).then_inc(s_te, 1)
                    act.wait_ge(s_ct, 1)
                    act.activation(kT[:, 0, TOK:KEYS], PS[:, 4, 0:P], ACT.Copy)
                    act.activation(kT[:, 1, TOK:KEYS], PS[:, 4, P:2 * P], ACT.Copy).then_inc(s_te, 1)
                    grp = 0
                    for t in range(NT):
                        z = zs[:, t % 2, :]
                        if t >= 2:
                            act.wait_ge(s_tp, t - 1)
                            act.wait_ge(s_rot, t - 1)
                        if t == 2:
                            act.wait_ge(s_co, 4 * 16)
                        for n in range(NGRP):
                            act.wait_ge(s_z, grp + 1)
                            src = PS[:, grp % 4, :]
                            if n == 0:
                                last = act.activation(z[:, SG:SG + QW], src[:, 0:QW], ACT.Copy)
                            elif n == 1:
                                act.activation(z[:, SG + QW:SG + 512], src[:, 0:KVW], ACT.Copy)
                                last = act.activation(vg[:, t, :], src[:, KVW:2 * KVW], ACT.Copy)
                            elif n == 2:
                                last = act.activation(z[:, SW:SW + QW], src[:, 0:QW], ACT.Copy)
                            elif n == 3:
                                act.activation(z[:, SW + QW:SW + 512], src[:, 0:KVW], ACT.Copy)
                                last = act.activation(vw[:, t, :], src[:, KVW:2 * KVW], ACT.Copy)
                            elif n == 4:
                                last = act.activation(z[:, 0:512], src, ACT.Copy)
                            elif n == 5:
                                act.activation(z[:, 512:768], src[:, 0:AW], ACT.Copy)
                                last = act.activation(va[:, t, :], src[:, AW:2 * AW], ACT.Copy)
                            else:
                                last = act.activation(ga[:, t, :], src[:, 0:AW], ACT.Sigmoid)
                            last.then_inc(s_ze, 1)
                            grp += 1
                        if t >= 1:
                            turned(t - 1)
                    turned(NT - 1)

                @block.gpsimd
                def _(pool):
                    for t in range(NT):
                        pool.wait_ge(s_rd, t + 1)
                        pool.tensor_tensor(small[:, 88:96], small[:, 96:104], minus_half[:, 0:8],
                                           ALU.pow).then_inc(s_rp, 1)

                @block.vector
                def _(dve):
                    link = chain(dve, s_zc)
                    ms, rs = small[:, 96:104], small[:, 88:96]

                    def turned(t):
                        dve.wait_ge(s_tp, t + 1)
                        for w in range(2):
                            dve.tensor_copy(qT[:, w, :, col(t)], PS[:, 4 + w, 0:QW].rearrange("p (j n) -> p j n", j=G))
                        dve.tensor_copy(kT[:, :, col(t)], PS[:, 4:6, QW:512]).then_inc(s_qm, 1)
                        dve.wait_ge(s_qs, t + 1)
                        dve.tensor_tensor(QQ[:, :, col(t)], QQ[:, :, col(t)],
                                          PS[:, 7, 0:2 * P].rearrange("p (f n) -> p f n", f=2), ALU.mult)\
                           .then_inc(s_qm, 1)

                    dve.wait_ge(s_par, 4 * 16)
                    for t in range(NT):
                        z = zs[:, t % 2, :]
                        qk = z[:, SG:SG + 512].rearrange("p (c e d) -> p c e d", e=2, d=HD)
                        dst = [hT[:, 4 * s:4 * s + 4, col(t)].rearrange("p c (e d) -> p c e d", d=HD) for s in range(2)]
                        if t >= 1:
                            turned(t - 1)
                        dve.wait_ge(s_ze, NGRP * (t + 1))
                        link(dve.tensor_tensor(dst[0], qk, qk, ALU.mult))
                        link(dve.tensor_reduce(ms, dst[0], AX.X, ALU.add))
                        dve.tensor_scalar(ms, ms, 1.0 / HD, EPS, ALU.mult, ALU.add).then_inc(s_rd, 1)
                        dve.wait_ge(s_rp, t + 1)
                        link(dve.tensor_tensor(qk, qk, rs.rearrange("p (c e) -> p c e", e=2).unsqueeze(3)
                                               .to_broadcast([P, 4, 2, HD]), ALU.mult))
                        out = dst[0] if t == 0 else qk
                        link(dve.tensor_tensor(out[:, 0:3, :, :], qk[:, 0:3, :, :],
                                               qkg[:, 0:1, :].unsqueeze(1).to_broadcast([P, 3, 2, HD]), ALU.mult))
                        link(dve.tensor_tensor(out[:, 3, :, :], qk[:, 3, :, :],
                                               qkg[:, 1:2, :].to_broadcast([P, 2, HD]), ALU.mult))
                        if t == 0:
                            dve.tensor_copy(hT[:, 4:8, col(0)], z[:, SW:SW + 512].rearrange("p (c n) -> p c n", c=4))\
                               .then_inc(s_rot, 1)
                            continue
                        for s, base in ((0, SG), (1, SW)):
                            src = z[:, base:base + 512].rearrange("p (c m b f) -> p c m b f", c=4, m=4, b=2)
                            o = hT[:, 4 * s:4 * s + 4, col(t)].rearrange("p c (m b f) -> p c m b f", m=4, b=2)
                            cs = cosT[:, t - 1:t, :, :].to_broadcast([P, 4, 4, 16])
                            sn = sinT[:, t - 1:t, :, :].to_broadcast([P, 4, 4, 16])
                            x1, x2 = src[:, :, :, 0, :], src[:, :, :, 1, :]
                            o1, o2 = o[:, :, :, 0, :], o[:, :, :, 1, :]
                            dve.tensor_tensor(o1, x1, cs, ALU.mult)
                            link(dve.tensor_tensor(o2, x2, cs, ALU.mult))
                            dve.tensor_tensor(x2, x2, sn, ALU.mult)
                            link(dve.tensor_tensor(x1, x1, sn, ALU.mult))
                            dve.tensor_tensor(o1, o1, x2, ALU.subtract)
                            ins = dve.tensor_tensor(o2, o2, x1, ALU.add)
                            if s == 1:
                                ins.then_inc(s_rot, 1)
                            else:
                                link(ins)
                    turned(NT - 1)

            s_as, s_am, s_ax, s_at, s_acv, s_aca, s_apv, s_aev, s_ach, s_es, s_esx = (
                lsem(n) for n in ("att_scores", "att_bias", "att_exp", "att_turned", "att_copy_vec", "att_copy_act",
                                  "att_pv", "att_out", "att_vec", "sink_shifted", "sink_exp"))
            s_side, s_free, s_hv, s_hm, s_wo, s_hg, s_st, s_hc, s_hx, s_hp, s_hq, s_so, s_fill, s_hf = (
                lsem(n) for n in ("side_products", "side_banks_read", "scan_vec", "scan_factors", "wout_load",
                                  "scan_pool", "state_load", "scan_out_copied", "scan_sq", "scan_mean", "scan_rstd",
                                  "state_stored", "spare_rows_filled", "gates_multiplied"))
            units = []
            for t in range(NT):
                for j in range(G):
                    for kv in range(KVH):
                        for wnd in range(2):
                            if t == 0:
                                keys, moff = [0], None
                            elif not wnd:
                                keys, moff = list(range(1, NT + 1)), None
                            else:
                                keys = ([t - 1] if t > 1 else []) + [t, NT] + ([t + 1] if t < NL else [])
                                moff = 0 if t > 1 else P
                            units.append((t, wnd, kv, j, keys, moff))
            U = len(units)
            GU = 2 * KVH
            negsink = small[:, 136:142]
            nbias = small[:, 144:144 + U]
            rsum = small[:, 208:208 + U]
            rinv = small[:, 272:272 + U]
            mxs = small[:, 336:336 + U]
            eshift = small[:, 400:404].rearrange("p (s h) -> p s h", s=2)
            esx = small[:, 408:412].rearrange("p (s h) -> p s h", s=2)

            def score_bank(u):
                return 2 * units[u][1]

            first_half = [(len(un[4]) + 1) // 2 for un in units]
            act_copies = [sum(len(un[4]) > 1 for un in units[:u]) for u in range(U + 1)]

            def in_group(u):
                return KVH * units[u][1] + units[u][2]

            def stat(a, u):
                n = (u // GU) * GU + in_group(u)
                return a[:, n:n + 1]

            NLEV = len(LEVELS) + 1
            STATE_STEPS = [(0, 0, None), (1, 0, None)] + [(d, i + 1 if d == 0 else NL - i, i)
                                                          for d in range(2) for i in range(NL - 1)]
            side_steps = []
            for lv in range(NLEV):
                for d in range(2):
                    side_steps += [("level", lv, d, t) for t in range(NT)]
                    side_steps.append(("mod_turn" if d else "mod_rows", MOD1 + lv))
            assert MOD1 + NLEV == 12
            for n in range(len(STATE_STEPS)):
                side_steps += [("keys", n), ("state", n)]
            side_steps += [("out", t) for t in range(NT)]
            NSIDE = len(side_steps)
            SIDE_START = 1
            side_at = {step: i for i, step in enumerate(side_steps)}

            def query_side(a, lv, d):
                if lv == 0:
                    return a
                h = LEVELS[lv - 1]
                if len(a.shape) == 2:
                    return a.rearrange("p (n two h) -> p n two h", two=2, h=h)[:, :, 1 - d, :]
                return a.rearrange("p a (n two h) -> p a n two h", two=2, h=h)[:, :, :, 1 - d, :]

            def sides_before(step, half):
                return min(NSIDE, max(0, 2 * (step - SIDE_START) + half))

            with nc.Block() as block:
                @block.sync
                def _(sp):
                    def load_mod2(n):
                        if n >= MOD1 + 2:
                            sp.wait_ge(s_side, side_at["mod_rows", n - 2] + 1)
                        sp.dma_start(modw2[:, n % 2, :, :],
                                     mod_w[layer, :, col(n, 512)].rearrange("(k p) n -> p k n", p=P))\
                          .then_inc(s_mw[n % 2], 16)
                    load_mod2(MOD1)
                    load_mod2(MOD1 + 1)
                    sp.wait_ge(s_hg, 4)
                    for d in range(2):
                        for h in range(AH):
                            f, r = h // 2, h % 2
                            sp.dma_start(Sv[64 * r:64 * r + 64, d, 0, f, 64 * r:64 * r + 64],
                                         state[0, layer, d, h]).then_inc(s_st, 16)
                    for n in range(MOD1 + 2, 12):
                        load_mod2(n)
                    sp.wait_ge(s_side, side_at["mod_rows", 11] + 1)
                    sp.dma_start(wout[:, :, :], w_out[layer].rearrange("(k p) n -> p k n", p=P)).then_inc(s_wo, 16)
                    spare = NS - 2 * NT
                    sp.dma_start(y_dram[2 * NT * P:, :].rearrange("(n p) c -> p n c", p=P),
                                 cst[:, 0:D].unsqueeze(1).to_broadcast([P, spare, D]), cond=(layer < 1))\
                      .then_inc(s_fill, 16)
                    sp.wait_ge(s_free, side_at["state", 1] + 1)
                    for d in range(2):
                        for h in range(AH):
                            f, r = h // 2, h % 2
                            sp.dma_start(new_state[0, layer, d, h], Sc[64 * r:64 * r + 64, d, f, :])\
                              .then_inc(s_so, 16)
                    sp.wait_ge(s_so, 8 * 16)
                    sp.wait_ge(s_fill, 16)

                @block.gpsimd
                def _(pool):
                    for d in range(2):
                        pool.memset(Am[:, d, :, :, :], 0.0).then_inc(s_hg, 1)
                    pool.memset(KF, 1.0).then_inc(s_hg, 1)
                    pool.memset(Sv, 0.0).then_inc(s_hg, 1)
                    flow = chain(pool, s_hf)
                    qq = QQ.rearrange("p f n -> p (f n)")
                    pool.wait_ge(s_hg, 4)

                    def factors(lv, d):
                        h = LEVELS[lv - 1]
                        qs, ks = (1, 0) if d == 0 else (0, 1)
                        last_pos = h - 1 if d == 0 else 0
                        nb = 2 * TOK // (2 * h)

                        def blocks(a):
                            return a.rearrange("p (n two h) -> p n two h", two=2, h=h)

                        m, q, kk, qf, kf = (blocks(a) for a in (
                            M[:, d, :, :].rearrange("p f n -> p (f n)"), qq,
                            KK[:, d, :, :].rearrange("p f n -> p (f n)"),
                            QF[:, d, :, :].rearrange("p f n -> p (f n)"),
                            KF[:, d, :, :].rearrange("p f n -> p (f n)")))

                        def block_product(side):
                            return qf[:, :, side, last_pos:last_pos + 1].to_broadcast([P, nb, h])

                        if lv == 1:
                            pool.wait_ge(s_hm, 2)
                        pool.wait_ge(s_side, side_at["level", lv - 1, d, NT - 1] + 1)
                        pool.tensor_tensor(m[:, :, qs, :], q[:, :, qs, :], qf[:, :, qs, :], ALU.mult)
                        pool.tensor_tensor(m[:, :, ks, :], kk[:, :, ks, :], kf[:, :, ks, :], ALU.mult).then_inc(s_hm, 1)
                        pool.wait_ge(s_hm, 2 * lv + d + 1)
                        flow(pool.tensor_tensor(kf[:, :, ks, :], kf[:, :, ks, :], block_product(qs), ALU.mult))
                        flow(pool.tensor_tensor(qf[:, :, qs, :], qf[:, :, qs, :], block_product(ks), ALU.mult))

                    for lv in range(1, NLEV):
                        for d in range(2):
                            factors(lv, d)
                    for d in range(2):
                        pool.wait_ge(s_side, side_at["level", NLEV - 1, d, NT - 1] + 1)
                        pool.tensor_tensor(M[:, d, :, :], QQ, QF[:, d, :, :], ALU.mult)
                        pool.tensor_tensor(KK[:, d, :, :], KK[:, d, :, :], KF[:, d, :, :], ALU.mult).then_inc(s_hm, 1)
                    pool.wait_ge(s_hp, 1)
                    pool.tensor_tensor(small[:, 88:88 + NT * AH], small[:, 112:112 + NT * AH],
                                       minus_half[:, 0:NT * AH], ALU.pow).then_inc(s_hq, 1)

                @block.tensor
                def _(pe):
                    def scores(u):
                        t, wnd, kv, j, keys, _ = units[u]
                        if u >= 2:
                            pe.wait_ge(s_ax, u - 1)
                        kv_rows = slice(64 * kv, 64 * kv + 64)
                        runs = []
                        for n, kt in enumerate(keys):
                            if runs and runs[-1][1] + runs[-1][2] == kt and n % 4:
                                runs[-1][2] += 1
                            else:
                                runs.append([n, kt, 1])
                        for n, kt, m in runs:
                            last = pe.matmul(PS[:, score_bank(u) + n // 4, (n % 4) * P:(n % 4 + m) * P],
                                             qT[kv_rows, wnd, j, col(t)], kT[kv_rows, wnd, kt * P:(kt + m) * P],
                                             start=True, stop=True)
                        last.then_inc(s_as, 1)

                    def turn(u):
                        pe.wait_ge(s_ax, u + 1)
                        if u >= 1:
                            pe.wait_ge(s_acv, u)
                            if act_copies[u]:
                                pe.wait_ge(s_aca, act_copies[u])
                        for n in range(len(units[u][4])):
                            bank, at = (3, n) if n < first_half[u] else (4, n - first_half[u])
                            last = pe.transpose(PS[:, bank, col(at)], pr[units[u][1]][:, col(n)], ident)
                        last.then_inc(s_at, 1)

                    def weigh(u):
                        t, wnd, kv, j, keys, _ = units[u]
                        pe.wait_ge(s_acv, u + 1)
                        if act_copies[u + 1]:
                            pe.wait_ge(s_aca, act_copies[u + 1])
                        g = u // GU
                        if u % GU == 0 and g >= 1:
                            pe.wait_ge(s_aev, g)
                        v = vw if wnd else vg
                        for n, kt in enumerate(keys):
                            last = pe.matmul(PS[:, 5, in_group(u) * HD:(in_group(u) + 1) * HD],
                                             prT[wnd][:, col(n)], v[:, kt, kv * HD:(kv + 1) * HD],
                                             start=(n == 0), stop=(n == len(keys) - 1))
                        last.then_inc(s_apv, 1)

                    def side(i):
                        kind, *at = side_steps[i]
                        if i >= 1:
                            pe.wait_ge(s_free, i)
                        if kind == "level":
                            lv, d, t = at
                            if t == 0:
                                pe.wait_ge(s_hm, 2 * lv + d + 1)
                            for h in range(AH):
                                f, r = h // 2, h % 2
                                k_op = KK if lv == 0 else M
                                rhs = QQ[64 * r:64 * r + 64, f, col(t)] if lv == 0 else \
                                    M[64 * r:64 * r + 64, d, f, col(t)]
                                last = pe.matmul(PS[:, 6 + r, col(f)], k_op[64 * r:64 * r + 64, d, f, col(t)], rhs,
                                                 start=True, stop=True)
                        elif kind == "mod_rows":
                            n, = at
                            pe.wait_ge(s_mw[n % 2], 16 * (n // 2 + 1))
                            for k in range(KC):
                                last = pe.matmul(PS[0:2, 6, :], condT[:, k, :], modw2[:, n % 2, k, :],
                                                 start=(k == 0), stop=(k == KC - 1))
                        elif kind == "mod_turn":
                            for m in range(4):
                                last = pe.transpose(PS[:, 6, 2 * m:2 * m + 2], modrow2[0:2, m // 2, col(m % 2)],
                                                    ident[0:2, 0:2])
                        elif kind == "keys":
                            d, t, _ = STATE_STEPS[at[0]]
                            pe.wait_ge(s_hm, 2 * NLEV + 1 + d)
                            for f in range(2):
                                last = pe.transpose(PS[:, 6, col(f)], KK[:, d, f, col(t)], ident)
                        elif kind == "state":
                            d, t, _ = STATE_STEPS[at[0]]
                            for f in range(2):
                                last = pe.matmul(PS[:, 6, col(f)], kout[:, col(f)], va[:, t, col(f)],
                                                 start=True, stop=True)
                        else:
                            t, = at
                            o = PS[:, 6, :]
                            first = True
                            for d in range(2):
                                if t > 0:
                                    step = t - 1 if d == 0 else NL - t
                                    for f in range(2):
                                        pe.matmul(o[:, col(f)], M[:, d, f, col(t)], Sv[:, d, step, f, :],
                                                  start=first, stop=False, skip_group_check=True)
                                        first = False
                                for h in range(AH):
                                    f, r = h // 2, h % 2
                                    last = pe.matmul(o[:, h * HD:(h + 1) * HD], Am[:, d, t, 2 * r + f, :],
                                                     va[:, t, h * HD:(h + 1) * HD], start=first,
                                                     stop=(d == 1 and h == AH - 1), skip_group_check=True)
                                    first = False
                        last.then_inc(s_side, 1)

                    for step in range(U + 2):
                        if step < U:
                            scores(step)
                        for i in range(sides_before(step, 0), sides_before(step, 1)):
                            side(i)
                        if 1 <= step <= U:
                            turn(step - 1)
                        for i in range(sides_before(step, 1), sides_before(step + 1, 0)):
                            side(i)
                        if step >= 2:
                            weigh(step - 2)
                    for i in range(sides_before(U + 2, 0), NSIDE):
                        side(i)

                @block.scalar
                def _(act):
                    def exponential(u):
                        t, wnd, kv, j, keys, moff = units[u]
                        n = len(keys) * P
                        act.wait_ge(s_am, u + 1)
                        if u >= 2:
                            act.wait_ge(s_at, u - 1)
                        b = score_bank(u)
                        src = PS[:, b:b + 2, :].rearrange("p b n -> p (b n)")[:, 0:n]
                        if moff is not None:
                            src = sm[:, 0:n]
                        act.activation(pr[wnd][:, 0:n], src, ACT.Exp, bias=stat(nbias, u), scale=SCALE,
                                       accum_out=stat(rsum, u)).then_inc(s_ax, 1)
                        if u % GU == GU - 1:
                            g = u // GU
                            act.wait_ge(s_es, g + 1)
                            act.activation(esx[:, g % 2, :], eshift[:, g % 2, :], ACT.Exp).then_inc(s_esx, 1)

                    def copy_turned(u):
                        n, m = len(units[u][4]) * P, first_half[u] * P
                        if n > m:
                            act.wait_ge(s_at, u + 1)
                            if u >= 2:
                                act.wait_ge(s_apv, u - 1)
                            act.activation(prT[units[u][1]][:, m:n], PS[:, 4, 0:n - m], ACT.Copy).then_inc(s_aca, 1)

                    def side(i):
                        kind, *at = side_steps[i]
                        if kind not in ("mod_rows", "keys", "out"):
                            return
                        act.wait_ge(s_side, i + 1)
                        if kind == "mod_rows":
                            act.activation(modrow2[0:2, :, :], PS[0:2, 6, :].rearrange("p (t n) -> p t n", t=2),
                                           ACT.Copy).then_inc(s_free, 1)
                        elif kind == "keys":
                            act.activation(kout, PS[:, 6, 0:AW], ACT.Copy).then_inc(s_free, 1)
                        else:
                            t, = at
                            act.activation(osum[:, t, :], PS[:, 6, 0:AW], ACT.Copy).then_inc(s_free, 1)
                            act.wait_ge(s_free, i + 1)
                            act.activation(osq[:, t, :], osum[:, t, :], ACT.Square).then_inc(s_hx, 1)

                    for step in range(U + 2):
                        if step < U:
                            exponential(step)
                        for i in range(sides_before(step, 0), sides_before(step, 1)):
                            side(i)
                        if 1 <= step <= U:
                            copy_turned(step - 1)
                        for i in range(sides_before(step, 1), sides_before(step + 1, 0)):
                            side(i)
                    for i in range(sides_before(U + 2, 0), NSIDE):
                        side(i)

                @block.vector
                def _(dve):
                    link = chain(dve, s_ach)
                    flow = chain(dve, s_hv)

                    def maximum(u):
                        t, wnd, kv, j, keys, moff = units[u]
                        n = len(keys) * P
                        b = score_bank(u)
                        src = PS[:, b:b + 2, :].rearrange("p b n -> p (b n)")[:, 0:n]
                        dve.wait_ge(s_as, u + 1)
                        if moff is None:
                            link(dve.tensor_reduce(stat(mxs, u), src, AX.X, ALU.max))
                        else:
                            if u >= 2:
                                dve.wait_ge(s_ax, u - 1)
                            link(dve.tensor_tensor_reduce(sm[:, 0:n], src, winmask[:, moff:moff + n],
                                                          1.0, 0.0, ALU.add, ALU.max, stat(mxs, u)))
                        if wnd:
                            h = kv * G + j
                            dve.tensor_scalar(stat(nbias, u), stat(mxs, u), -SCALE, negsink[:, h:h + 1],
                                              ALU.mult, ALU.min).then_inc(s_am, 1)
                        else:
                            dve.tensor_scalar(stat(nbias, u), stat(mxs, u), -SCALE, None, ALU.mult)\
                               .then_inc(s_am, 1)
                        if u % GU == GU - 1:
                            g = u // GU
                            dve.wait_ge(s_am, u + 1)
                            dve.tensor_tensor(eshift[:, g % 2, :], nbias[:, g * GU + KVH:(g + 1) * GU],
                                              sink[:, :].rearrange("p (k j) -> p j k", k=KVH)[:, j, :], ALU.add)\
                               .then_inc(s_es, 1)

                    def copy_turned(u):
                        m = first_half[u] * P
                        dve.wait_ge(s_at, u + 1)
                        if u >= 2:
                            dve.wait_ge(s_apv, u - 1)
                        dve.tensor_copy(prT[units[u][1]][:, 0:m], PS[:, 3, 0:m]).then_inc(s_acv, 1)

                    def outputs(g):
                        t, _, _, j = units[g * GU][0:4]
                        den = rsum[:, g * GU:(g + 1) * GU]
                        inv = rinv[:, g * GU:(g + 1) * GU]
                        dve.wait_ge(s_apv, (g + 1) * GU)
                        dve.wait_ge(s_esx, g + 1)
                        link(dve.tensor_tensor(den[:, KVH:], den[:, KVH:], esx[:, g % 2, :], ALU.add))
                        link(dve.reciprocal(inv, den))
                        dve.tensor_tensor(oall[:, t, AW:D].rearrange("p (a j d) -> p j a d", a=GU, j=G)[:, j],
                                          PS[:, 5, 0:GU * HD].rearrange("p (a d) -> p a d", a=GU),
                                          inv.unsqueeze(2).to_broadcast([P, GU, HD]), ALU.mult)\
                           .then_inc(s_aev, 1)

                    def start_scan(d):
                        for f in range(2):
                            flow(dve.tensor_scalar(QF[:, d, f, :], QF[:, d, f, :], olb[:, d, f:f + 1],
                                                   lb[:, d, f:f + 1], ALU.mult, ALU.add))
                            flow(dve.tensor_scalar(QF[:, d, f, :], QF[:, d, f, :], TINY, None, ALU.max))
                            ins = dve.tensor_scalar(KK[:, d, f, :], KK[:, d, f, :], olb[:, d, f:f + 1], None, ALU.mult)
                        ins.then_inc(s_hm, 1)

                    def side(i):
                        kind, *at = side_steps[i]
                        if kind not in ("level", "mod_turn", "state"):
                            return
                        dve.wait_ge(s_side, i + 1)
                        if kind == "level":
                            lv, d, t = at
                            if (lv, t) == (0, 0):
                                dve.wait_ge(s_hg, d + 1)
                            mask = query_side(levelmask[:, d, lv, :], lv, d).unsqueeze(1)
                            dve.copy_predicated(
                                query_side(Am[:, d, t, :, :], lv, d),
                                mask.to_broadcast([P, 4] + list(mask.shape[2:])),
                                query_side(PS[:, 6:8, 0:2 * P], lv, d)).then_inc(s_free, 1)
                        elif kind == "mod_turn":
                            n, = at
                            dve.tensor_tensor(modc[:, 4 * n:4 * n + 4, :],
                                              PS[:, 6, 0:8].rearrange("p (m s) -> p m s", s=2),
                                              small[:, 4 * n:4 * n + 4].unsqueeze(2).to_broadcast([P, 4, 2]), ALU.add)\
                               .then_inc(s_free, 1)
                            if n == 9:
                                dve.wait_ge(s_free, i + 1)
                                flow(dve.tensor_scalar(scale2[:, :, :], modc[:, 4 * KC:5 * KC, :], 1.0, None, ALU.add))
                                flow(dve.tensor_tensor(scale2[:, :, :], scale2[:, :, :],
                                                       small[:, 56:56 + KC].unsqueeze(2).to_broadcast([P, KC, 2]),
                                                       ALU.mult))
                        else:
                            d, t, step = STATE_STEPS[at[0]]
                            edge = t * P + (P - 1 if d == 0 else 0)
                            dve.wait_ge(s_free, i)
                            if at[0] == 0:
                                dve.wait_ge(s_st, 8 * 16)
                                dve.wait_ge(s_hm, 2 * NLEV + 2)
                            for r in range(2):
                                rows_r = slice(64 * r, 64 * r + 64)
                                if t == 0:
                                    ins = dve.tensor_copy(Sc[rows_r, d, :, :],
                                                          PS[rows_r, 6, 0:2 * P].rearrange("p (f n) -> p f n", f=2)
                                                          [:, :, 64 * r:64 * r + 64])
                                    continue
                                for f in range(2):
                                    ins = dve.scalar_tensor_tensor(
                                        Sv[rows_r, d, step + 1, f, rows_r], Sv[rows_r, d, step, f, rows_r],
                                        QF[rows_r, d, f, edge:edge + 1],
                                        PS[rows_r, 6, f * P + 64 * r:f * P + 64 * r + 64], ALU.mult, ALU.add)
                            ins.then_inc(s_free, 1)

                    link(dve.tensor_scalar(negsink, sink[:, :], -1.0, None, ALU.mult))
                    for step in range(U + 3):
                        if step < U:
                            maximum(step)
                        if step >= 3 and (step - 3) % GU == GU - 1:
                            outputs((step - 3) // GU)
                        for i in range(sides_before(step, 0), sides_before(step, 1)):
                            side(i)
                        if 1 <= step <= U:
                            copy_turned(step - 1)
                        if step < 2:
                            start_scan(step)
                        for i in range(sides_before(step, 1), sides_before(step + 1, 0)):
                            side(i)
                    for i in range(sides_before(U + 3, 0), NSIDE):
                        side(i)
                    ms = small[:, 112:112 + NT * AH]
                    rs = small[:, 88:88 + NT * AH].rearrange("p (t a) -> p t a", t=NT)
                    dve.wait_ge(s_hx, NT)
                    flow(dve.tensor_reduce(ms, osq.rearrange("p t (a d) -> p (t a) d", d=HD), AX.X, ALU.add))
                    dve.tensor_scalar(ms, ms, 1.0 / HD, EPS, ALU.mult, ALU.add).then_inc(s_hp, 1)
                    og = osum.rearrange("p t (a d) -> p (t a) d", d=HD)
                    flow(dve.tensor_tensor(og, og, ang[:, :].unsqueeze(1).to_broadcast([P, NT * AH, HD]), ALU.mult))
                    flow(dve.tensor_tensor(osum, osum, ga, ALU.mult))
                    dve.wait_ge(s_hq, 1)
                    flow(dve.tensor_tensor(oall[:, :, 0:AW].rearrange("p t (a d) -> p t a d", d=HD),
                                           osum.rearrange("p t (a d) -> p t a d", d=HD),
                                           rs.unsqueeze(3).to_broadcast([P, NT, AH, HD]), ALU.mult))

            s_gb, s_gbe, s_ot, s_ote, s_y, s_yp, s_yv = (
                lsem(n) for n in ("gate_rows", "gate_rows_evac", "o_turned", "o_turned_evac", "y_done", "y_gated",
                                  "y_added"))

            def gate_rows(pe, columns, bank0, s_sig):
                for cond in range(2):
                    for k in range(KC):
                        last = pe.matmul(PS[:, bank0 + 2 * cond + k // 4, col(k % 4)],
                                         columns[:, k, cond:cond + 1].to_broadcast([P, P]), ident,
                                         start=True, stop=True)
                last.then_inc(s_sig, 1)

            with nc.Block() as block:
                @block.tensor
                def _(pe):
                    gate_rows(pe, modc[:, 2 * KC:3 * KC, :], 4, s_gb)
                    pe.wait_ge(s_wo, 16)

                    def turn(t):
                        if t >= 2:
                            pe.wait_ge(s_ote, t - 1)
                        for k in range(KC):
                            last = pe.transpose(PS[:, 2 * (t % 2) + k // 4, col(k % 4)], oall[:, t, col(k)], ident)
                        last.then_inc(s_ot, 1)

                    turn(0)
                    for t in range(NT):
                        if t + 1 < NT:
                            turn(t + 1)
                        pe.wait_ge(s_ote, t + 1)
                        if t < 2:
                            pe.wait_ge(s_gbe, 1)
                        else:
                            pe.wait_ge(s_yp, t - 1)
                        for b in range(2):
                            for k in range(KC):
                                last = pe.matmul(PS[:, 4 + 2 * (t % 2) + b, :], oT[:, t % 2, k, :],
                                                 wout[:, k, col(b, 512)], start=(k == 0), stop=(k == KC - 1))
                        last.then_inc(s_y, 1)

                @block.scalar
                def _(act):
                    act.wait_ge(s_gb, 1)
                    act.activation(g1b[:, :, :].rearrange("p s n -> p (s n)"),
                                   PS[:, 4:8, :].rearrange("p b n -> p (b n)"), ACT.Copy).then_inc(s_gbe, 1)
                    for t in range(NT):
                        act.wait_ge(s_ot, t + 1)
                        if t >= 2:
                            act.wait_ge(s_y, t - 1)
                        act.activation(oT[:, t % 2, :, :].rearrange("p k n -> p (k n)"),
                                       PS[:, 2 * (t % 2):2 * (t % 2) + 2, :].rearrange("p b n -> p (b n)"),
                                       ACT.Copy).then_inc(s_ote, 1)

                @block.vector
                def _(dve):
                    dve.wait_ge(s_gbe, 1)
                    for t in range(NT):
                        dve.wait_ge(s_y, t + 1)
                        if t >= 2:
                            dve.wait_ge(s_yv, t - 1)
                        dve.tensor_tensor(prod[:, t % 2, :],
                                          PS[:, 4 + 2 * (t % 2):6 + 2 * (t % 2), :].rearrange("p b n -> p (b n)"),
                                          g1b[:, 1 if t else 0, :], ALU.mult).then_inc(s_yp, 1)
                        dve.wait_ge(s_yp, t + 1)
                        dve.tensor_tensor(x[:, t, :], x[:, t, :], prod[:, t % 2, :], ALU.add).then_inc(s_yv, 1)

            (s_n2q, s_n2m, s_n2p, s_n2x, s_n2r, s_n2e, s_n2h, s_n2t, s_n2c, s_hst, s_rw, s_rl, s_rg, s_rv, s_cnt,
             s_tab, s_hot, s_slt) = (
                lsem(n) for n in ("norm2_squares", "norm2_mean", "norm2_rstd", "norm2_scaled", "rows_made",
                                  "rows_evac", "norm2_rows", "norm2_turned", "norm2_turned_evac", "h_stored",
                                  "router_load", "router_logits", "router_sigmoid", "router_vec", "pair_counts",
                                  "tile_tables", "slots_one_hot", "slot_tokens"))
            (s_ga0, s_ga1, s_ewg0, s_ewg1, s_ewd0, s_ewd1, s_ext, s_exe, s_eg, s_esg, s_et1, s_eh, s_etr, s_etc, s_ey, s_eye, s_eys0, s_eys1,
             s_cga, s_cgb, s_cm, s_ca, s_all) = (
                lsem(n) for n in ("rows_gathered0", "rows_gathered1", "gate_up_load0", "gate_up_load1", "down_load0", "down_load1", "rows_turned2",
                                  "rows_turned_evac", "gate_up_done", "gate_sigmoid", "gate_times", "act_done",
                                  "act_turned", "act_turned_evac", "down_done", "down_evac", "y_stored0", "y_stored1",
                                  "pair_gather0", "pair_gather1", "combine_vec", "first_weighted",
                                  "all_stored"))
            s_ga, s_ewg, s_ewd, s_eys, s_cg = [s_ga0, s_ga1], [s_ewg0, s_ewg1], [s_ewd0, s_ewd1], [s_eys0, s_eys1], [s_cga, s_cgb]
            ss, ms, rs = small[:, 64:64 + NT], small[:, 72:72 + NT], small[:, 80:80 + NT]
            nte = NT * NE
            sc, sel = rt[:, 0:nte], rt[:, nte:2 * nte]
            rk, top2, tv = (rt[:, 240 + nte * n:240 + nte * (n + 1)] for n in range(3))
            gs, grk, gm = (rt[:, 520 + 20 * n:540 + 20 * n] for n in range(3))
            den, inv = rt[:, 600:605], rt[:, 608:613]
            before = rc[:, RC_BEFORE:RC_BEFORE + P]
            all_ones = rc[:, RC_ONES:RC_ONES + P]
            hot_place = rt[:, 1600:1600 + 2 * NT * P].rearrange("p (n s) -> p n s", s=P)
            hot_tile = rt[:, 2900:2900 + 2 * NT * NS].rearrange("p (n j) -> p n j", j=NS)

            def load_gate_up(sp, j, par, least):
                e = sp.value_load(tile_expert[0:1, bass.ds(j, 1)], min_val=0, max_val=NE - 1)
                used = sp.value_load(tile_used[0:1, bass.ds(j, 1)], min_val=0, max_val=1)
                if least >= 2:
                    sp.wait_ge(s_eg, j - 1)
                sp.dma_start(exps[:, par, 0:4096].rearrange("p (k n) -> p k n", k=KC),
                             w_gate_up[layer, e].rearrange("(k p) n -> p k n", p=P), cond=used)\
                  .then_inc(s_ewg[par], 16)

            def load_down(sp, j, par, least):
                e = sp.value_load(tile_expert[0:1, bass.ds(j, 1)], min_val=0, max_val=NE - 1)
                used = sp.value_load(tile_used[0:1, bass.ds(j, 1)], min_val=0, max_val=1)
                if least >= 2:
                    sp.wait_ge(s_ey, j - 1)
                sp.dma_start(exps[:, par, 4096:6144].rearrange("p (k n) -> p k n", k=2),
                             w_down[layer, e].rearrange("(k p) n -> p k n", p=P), cond=used)\
                  .then_inc(s_ewd[par], 16)

            def by_expert(a):
                return a.rearrange("p (t e) -> p t e", e=NE)

            with nc.Block() as block:
                @block.sync
                def _(sp):
                    sp.dma_start(rw, router_w.rearrange("(k p) n -> p k n", p=P)).then_inc(s_rw, 16)
                    sp.dma_start(rc, route_consts).then_inc(s_rw, 16)
                    for t in range(NT):
                        sp.wait_ge(s_n2h, 2 * t + 2)
                        sp.dma_start(h_dram[col(t), :], h2[:, t, :]).then_inc(s_hst, 16)
                    sp.wait_ge(s_tab, 1)
                    for j in range(2):
                        load_gate_up(sp, j, j, j)
                        load_down(sp, j, j, j)
                    sp.wait_ge(s_hst, NT * 16)

                @block.gpsimd
                def _(pool):
                    pool.wait_ge(s_n2m, 1)
                    pool.tensor_tensor(rs, ms, minus_half[:, 0:NT], ALU.pow).then_inc(s_n2p, 1)

                @block.scalar
                def _(act):
                    for t in range(NT):
                        if t >= 1:
                            act.wait_ge(s_n2q, t)
                        act.activation(h2[:, NT - 1, :], x[:, t, :], ACT.Square,
                                       accum_out=ss[:, t:t + 1]).then_inc(s_n2q, 1)
                    act.wait_ge(s_n2p, 1)
                    act.wait_ge(s_n2q, NT)
                    for t in range(NT):
                        act.activation(h2[:, t, :], x[:, t, :], ACT.Copy, scale=rs[:, t:t + 1]).then_inc(s_n2x, 1)
                    for t in range(NT):
                        act.wait_ge(s_n2t, t + 1)
                        act.activation(hT[:, :, col(t)],
                                       PS[:, 2 * (t % 2):2 * (t % 2) + 2, :].rearrange("p b (k n) -> p (b k) n", k=4),
                                       ACT.Copy).then_inc(s_n2c, 1)
                    act.wait_ge(s_rl, 1)
                    act.activation(sc, PS[:, 4, 0:nte], ACT.Sigmoid).then_inc(s_rg, 1)

                @block.tensor
                def _(pe):
                    gate_rows(pe, scale2[:, :, :], 4, s_n2r)
                    gate_rows(pe, modc[:, 3 * KC:4 * KC, :], 0, s_n2r)
                    pe.wait_ge(s_n2e, 1)
                    gate_rows(pe, modc[:, 5 * KC:6 * KC, :], 4, s_n2r)
                    pe.wait_ge(s_n2e, 3)
                    pe.wait_ge(s_rw, 2 * 16)
                    for t in range(NT + 1):
                        if t < NT:
                            pe.wait_ge(s_n2h, 2 * t + 2)
                            if t >= 2:
                                pe.wait_ge(s_n2c, t - 1)
                            for k in range(KC):
                                last = pe.transpose(PS[:, 2 * (t % 2) + k // 4, col(k % 4)], h2[:, t, col(k)], ident)
                            last.then_inc(s_n2t, 1)
                        if t >= 1:
                            pe.wait_ge(s_n2c, t)
                            for k in range(KC):
                                last = pe.matmul(PS[:, 4, (t - 1) * NE:t * NE], hT[:, k, col(t - 1)], rw[:, k, :],
                                                 start=(k == 0), stop=(k == KC - 1))
                    last.then_inc(s_rl, 1)
                    pe.wait_ge(s_cnt, 1)
                    pe.matmul(PS[:, 5, 0:nte], before, top2, start=True, stop=True)
                    pe.matmul(PS[:, 5, nte:2 * nte], all_ones, top2, start=True, stop=True).then_inc(s_rl, 1)
                    pe.wait_ge(s_hot, 1)
                    for n in range(2 * NT):
                        last = pe.matmul(PS[:, 6, 0:NS], hot_place[:, n, :], hot_tile[:, n, :],
                                         start=(n == 0), stop=(n == 2 * NT - 1))
                    last.then_inc(s_slt, 1)

                @block.vector
                def _(dve):
                    link = chain(dve, s_rv)
                    for n, (dst, bank0) in enumerate(((arow, 4), (brow, 0), (g2b, 4))):
                        dve.wait_ge(s_n2r, n + 1)
                        dve.tensor_copy(dst.rearrange("p s n -> p (s n)"),
                                        PS[:, bank0:bank0 + 4, :].rearrange("p b n -> p (b n)")).then_inc(s_n2e, 1)
                        if n == 1:
                            dve.wait_ge(s_n2q, NT)
                            dve.tensor_scalar(ms, ss, 1.0 / D, EPS, ALU.mult, ALU.add).then_inc(s_n2m, 1)
                    dve.wait_ge(s_n2e, 3)
                    for t in range(NT):
                        cond = 1 if t else 0
                        dve.wait_ge(s_n2x, t + 1)
                        dve.tensor_tensor(h2[:, t, :], h2[:, t, :], arow[:, cond, :], ALU.mult).then_inc(s_n2h, 1)
                        dve.wait_ge(s_n2h, 2 * t + 1)
                        dve.tensor_tensor(h2[:, t, :], h2[:, t, :], brow[:, cond, :], ALU.add).then_inc(s_n2h, 1)

                    def rank(out, val, n):
                        def four(a):
                            return a.rearrange("p (n i j) -> p n i j", i=4, j=4)
                        other = val.rearrange("p (n j) -> p n j", j=4).unsqueeze(2).to_broadcast([P, n, 4, 4])
                        mine = val.rearrange("p (n j) -> p n j", j=4).unsqueeze(3).to_broadcast([P, n, 4, 4])
                        gt, eq = rt[:, 1024:1024 + 16 * n], rt[:, 2048:2048 + 16 * n]
                        dve.tensor_tensor(four(gt), other, mine, ALU.is_gt)
                        link(dve.tensor_tensor(four(eq), other, mine, ALU.is_equal))
                        link(dve.tensor_tensor(eq.rearrange("p (n k) -> p n k", k=16), eq.rearrange("p (n k) -> p n k", k=16),
                                               ltmask.unsqueeze(1).to_broadcast([P, n, 16]), ALU.mult))
                        link(dve.tensor_tensor(gt, gt, eq, ALU.add))
                        link(dve.tensor_reduce(out, gt.rearrange("p (m j) -> p m j", j=4), AX.X, ALU.add))

                    dve.wait_ge(s_rg, 1)
                    link(dve.tensor_tensor(by_expert(sel), by_expert(sc),
                                           rbias[:, :].unsqueeze(1).to_broadcast([P, NT, NE]), ALU.add))
                    rank(rk, sel, NT * NG)
                    link(dve.tensor_scalar(top2, rk, 2.0, None, ALU.is_lt))
                    link(dve.tensor_tensor(tv, sel, top2, ALU.mult))
                    link(dve.tensor_reduce(gs, tv.rearrange("p (m j) -> p m j", j=EPG), AX.X, ALU.add))
                    rank(grk, gs, NT)
                    link(dve.tensor_scalar(gm, grk, 1.0, None, ALU.is_lt))
                    dve.tensor_tensor(top2.rearrange("p (m j) -> p m j", j=EPG),
                                      top2.rearrange("p (m j) -> p m j", j=EPG),
                                      gm.unsqueeze(2).to_broadcast([P, NT * NG, EPG]), ALU.mult).then_inc(s_cnt, 1)
                    dve.wait_ge(s_cnt, 1)
                    link(dve.tensor_tensor(tv, sc, top2, ALU.mult))
                    link(dve.tensor_reduce(den, by_expert(tv), AX.X, ALU.add))
                    link(dve.reciprocal(inv, den))
                    link(dve.tensor_tensor(by_expert(tv), by_expert(tv), inv.unsqueeze(2).to_broadcast([P, NT, NE]),
                                           ALU.mult))
                    nt, end, base, on = (rt[:, 640 + 16 * n:656 + 16 * n] for n in range(4))
                    slots, tmp = rt[:, 720:720 + nte], rt[:, 800:800 + nte]
                    dve.wait_ge(s_rl, 2)
                    run = rt[:, 880:880 + (NT + 1) * NE]
                    link(dve.memset(run[:, 0:NE], 0.0))
                    for t in range(NT):
                        link(dve.tensor_tensor(run[:, (t + 1) * NE:(t + 2) * NE], run[:, t * NE:(t + 1) * NE],
                                               PS[:, 5, nte + t * NE:nte + (t + 1) * NE], ALU.add))
                    cnt = run[:, nte:nte + NE]
                    link(dve.tensor_scalar(nt, cnt, 0.0, None, ALU.is_gt))
                    for m in range(1, NT):
                        link(dve.scalar_tensor_tensor(nt, cnt, float(P * m), nt, ALU.is_gt, ALU.add))
                    link(dve.memset(on, 1.0))
                    link(dve.tensor_tensor_scan(end, on, nt, 0.0, ALU.mult, ALU.add))
                    cmp = rt[:, 1024:1024 + NS * NE].rearrange("p (j e) -> p j e", e=NE)
                    link(dve.tensor_tensor(cmp, rc[:, RC_TILE:RC_TILE + NS].unsqueeze(2).to_broadcast([P, NS, NE]),
                                           end.unsqueeze(1).to_broadcast([P, NS, NE]), ALU.is_ge))
                    ef = rt[:, 1500:1500 + NS]
                    link(dve.tensor_reduce(ef, cmp, AX.X, ALU.add))
                    ef_used = rt[:, 1540:1540 + NS]
                    link(dve.tensor_scalar(ef_used, ef, float(NE), None, ALU.is_lt))
                    dve.tensor_copy(tile_used, ef_used)
                    looped_f = rt[:, 1580:1581]
                    link(dve.tensor_reduce(looped_f, ef_used[:, 3:NS].rearrange("p (n two) -> p n two", two=2)[:, :, 0],
                                           AX.X, ALU.add))
                    link(dve.tensor_scalar(looped_f, looped_f, 2.0, None, ALU.mult))
                    dve.tensor_copy(tiles_looped, looped_f)
                    link(dve.tensor_scalar(ef, ef, float(NE - 1), None, ALU.min))
                    dve.tensor_copy(tile_expert, ef).then_inc(s_tab, 1)
                    link(dve.tensor_tensor(base, end, nt, ALU.subtract))
                    link(dve.tensor_scalar(base, base, float(P), None, ALU.mult))
                    link(dve.tensor_tensor(by_expert(slots), PS[:, 5, 0:nte].rearrange("p (t e) -> p t e", e=NE),
                                           base.unsqueeze(1).to_broadcast([P, NT, NE]), ALU.add))
                    link(dve.tensor_tensor(slots, slots, run[:, 0:nte], ALU.add))
                    link(dve.scalar_tensor_tensor(tmp, slots, 1.0, top2, ALU.add, ALU.mult))
                    link(dve.tensor_reduce(slot_f[:, 0, :], by_expert(tmp), AX.X, ALU.max))
                    link(dve.tensor_scalar(slot_f[:, 0, :], slot_f[:, 0, :], -1.0, None, ALU.add))
                    far = float(NS * P)
                    link(dve.tensor_scalar(tmp, slots, -1.0, far, ALU.mult, ALU.add))
                    link(dve.tensor_tensor(tmp, tmp, top2, ALU.mult))
                    link(dve.tensor_reduce(slot_f[:, 1, :], by_expert(tmp), AX.X, ALU.max))
                    link(dve.tensor_scalar(slot_f[:, 1, :], slot_f[:, 1, :], -1.0, far, ALU.mult, ALU.add))
                    flat = slot_f.rearrange("p c t -> p (c t)")
                    wide = [P, 2 * NT, NS]
                    tiles = rc[:, RC_TILE:RC_TILE + NS].unsqueeze(1).to_broadcast(wide)
                    in_tiles, tile_n, place = (rt[:, 3200 + 16 * n:3200 + 16 * n + 2 * NT] for n in range(3))
                    link(dve.tensor_scalar(in_tiles, flat, 1.0 / P, None, ALU.mult))
                    link(dve.tensor_tensor(hot_tile, in_tiles.unsqueeze(2).to_broadcast(wide), tiles, ALU.is_ge))
                    link(dve.tensor_reduce(tile_n, hot_tile, AX.X, ALU.add))
                    link(dve.tensor_scalar(tile_n, tile_n, -1.0, None, ALU.add))
                    link(dve.scalar_tensor_tensor(place, tile_n, -float(P), flat, ALU.mult, ALU.add))
                    dve.tensor_tensor(hot_place, rc[:, RC_IOTA:RC_IOTA + P].unsqueeze(1).to_broadcast([P, 2 * NT, P]),
                                      place.unsqueeze(2).to_broadcast([P, 2 * NT, P]), ALU.is_equal)
                    link(dve.tensor_tensor(hot_tile, tile_n.unsqueeze(2).to_broadcast(wide), tiles, ALU.is_equal))
                    tokens = rc[:, RC_TOKEN:RC_TOKEN + NT]
                    by_pair = hot_tile.rearrange("p (c t) j -> p c t j", c=2)
                    for cc in range(2):
                        ins = dve.tensor_tensor(by_pair[:, cc], by_pair[:, cc],
                                                tokens.unsqueeze(2).to_broadcast([P, NT, NS]), ALU.mult)
                    ins.then_inc(s_hot, 1)
                    dve.tensor_copy(slot_i, slot_f)
                    for cc in range(2):
                        link(dve.tensor_tensor(by_expert(tmp), by_expert(slots),
                                               slot_f[:, cc, :].unsqueeze(2).to_broadcast([P, NT, NE]), ALU.is_equal))
                        link(dve.tensor_tensor(tmp, tmp, tv, ALU.mult))
                        link(dve.tensor_reduce(wpair[:, cc, :], by_expert(tmp), AX.X, ALU.add))
                    dve.wait_ge(s_slt, 1)
                    dve.tensor_copy(slot_token[:, 0:NS], PS[:, 6, 0:NS])
                    dve.memset(slot_token[:, NS:NS + 1], 0)

            LAST = NS - 1
            assert NS % 2 == 1

            def load_last(eng):
                return eng.value_load(tiles_looped[0:1, 0:1], min_val=0, max_val=LAST - 2) + 2

            def over_tiles(eng, step, first):
                for j in range(first, 3):
                    step(j, j % 2, j)
                with eng.Fori(0, (LAST - 2) // 2) as it:
                    used = eng.value_load(tile_used[0:1, bass.ds(it * 2 + 3, 1)], min_val=0, max_val=1)
                    with eng.If(used > 0):
                        step(it * 2 + 3, 1, 3)
                        step(it * 2 + 4, 0, 3)

            with nc.Block() as block:
                @block.sync
                def _(sp):
                    def step(j, par, least):
                        load_gate_up(sp, j, par, least)
                        load_down(sp, j - 1, 1 - par, least - 1)
                    load_gate_up(sp, 2, 0, 2)
                    over_tiles(sp, step, 3)
                    load_down(sp, load_last(sp), 0, 2)

                @block.gpsimd
                def _(pool):
                    def gather(j):
                        if j >= 2:
                            pool.wait_ge(s_ext, j - 1)
                        pool.indirect_dma_start(out=hg[:, j % 2, :], out_offset=None, in_=h_dram,
                                                in_offset=bass.IndirectOffsetOnAxis(slot_token[:, j:j + 1], 0))\
                            .then_inc(s_ga[j % 2], 16)

                    for j in range(4):
                        gather(j)
                    for j in range(3, NS, 2):
                        used = pool.value_load(tile_used[0:1, j:j + 1], min_val=0, max_val=1)
                        with pool.If(used > 0):
                            gather(j + 1)
                            gather(j + 2)
                    pool.wait_ge(s_all, 2)
                    for t in range(NT):
                        if t >= 2:
                            pool.wait_ge(s_cm, 3 * (t - 1))
                        for cc in range(2):
                            pool.indirect_dma_start(out=yab[:, t % 2, cc, :], out_offset=None, in_=y_dram,
                                                    in_offset=bass.IndirectOffsetOnAxis(slot_i[:, cc, t:t + 1], 0))\
                                .then_inc(s_cg[t % 2], 16)
                    pool.wait_ge(s_cg[0], 32 * ((NT + 1) // 2))
                    pool.wait_ge(s_cg[1], 32 * (NT // 2))

                @block.tensor
                def _(pe):
                    def rows(j, par, least):
                        pe.wait_ge(s_ga[par], (j - par) * 8 + 16)
                        if least >= 1:
                            pe.wait_ge(s_exe, j)
                        for k in range(KC):
                            last = pe.transpose(PS[:, k // 4, col(k % 4)], hg[:, par, col(k)], ident)
                        last.then_inc(s_ext, 1)

                    def gate_up(j, par, least):
                        pe.wait_ge(s_exe, j + 1)
                        pe.wait_ge(s_ewg[par], (j - par) * 8 + 16)
                        if least >= 2:
                            pe.wait_ge(s_eh, j - 1)
                        w = exps[:, par, 0:4096].rearrange("p (k n) -> p k n", k=KC)
                        for k in range(KC):
                            last = pe.matmul(PS[:, 2 + par, :], hgT[:, par, k, :], w[:, k, :],
                                             start=(k == 0), stop=(k == KC - 1))
                        last.then_inc(s_eg, 1)

                    def turn(j, par, least):
                        pe.wait_ge(s_eh, j + 1)
                        for f in range(2):
                            last = pe.transpose(PS[:, 4 + par, col(f)], ha[:, par, col(f)], ident)
                        last.then_inc(s_etr, 1)

                    def down(j, par, least):
                        pe.wait_ge(s_etc, j + 1)
                        pe.wait_ge(s_ewd[par], (j - par) * 8 + 16)
                        if least >= 1:
                            pe.wait_ge(s_eye, j)
                        w = exps[:, par, 4096:6144].rearrange("p (k n) -> p k n", k=2)
                        for b in range(2):
                            for f in range(2):
                                last = pe.matmul(PS[:, 6 + b, :], haT[:, par, col(f)], w[:, f, col(b, 512)],
                                                 start=(f == 0), stop=(f == 1))
                        last.then_inc(s_ey, 1)

                    def step(j, par, least):
                        gate_up(j, par, least)
                        if least >= 1:
                            turn(j - 1, 1 - par, least - 1)
                        rows(j + 1, 1 - par, least + 1)
                        if least >= 1:
                            down(j - 1, 1 - par, least - 1)
                    rows(0, 0, 0)
                    over_tiles(pe, step, 0)
                    last = load_last(pe)
                    turn(last, 0, 2)
                    down(last, 0, 2)

                @block.scalar
                def _(act):
                    def rows_evac(j, par, least):
                        act.wait_ge(s_ext, j + 1)
                        if least >= 2:
                            act.wait_ge(s_eg, j - 1)
                        act.activation(hgT[:, par, :, :].rearrange("p k n -> p (k n)"),
                                       PS[:, 0:2, :].rearrange("p b n -> p (b n)"), ACT.Copy).then_inc(s_exe, 1)

                    def store(j, par):
                        act.wait_ge(s_eye, j + 1)
                        act.dma_start(y_dram[bass.ds(j * P, P), :], ys[:, par, :]).then_inc(s_eys[par], 16)

                    def step(j, par, least):
                        act.wait_ge(s_eg, j + 1)
                        if least >= 2:
                            act.wait_ge(s_eh, j - 1)
                        act.activation(sg[:, par, :], PS[:, 2 + par, 0:DE], ACT.Sigmoid).then_inc(s_esg, 1)
                        if least >= 1:
                            act.wait_ge(s_etr, j)
                            if least >= 3:
                                act.wait_ge(s_ey, j - 2)
                            act.activation(haT[:, 1 - par, :], PS[:, 5 - par, 0:DE], ACT.Copy).then_inc(s_etc, 1)
                        rows_evac(j + 1, 1 - par, least + 1)
                        if least >= 2:
                            store(j - 2, par)
                    rows_evac(0, 0, 0)
                    over_tiles(act, step, 0)
                    last = load_last(act)
                    act.wait_ge(s_etr, last + 1)
                    act.activation(haT[:, 0, :], PS[:, 4, 0:DE], ACT.Copy).then_inc(s_etc, 1)
                    store(last - 1, 1)
                    store(last, 0)
                    act.wait_ge(s_eys[0], last * 8 + 16)
                    act.activation(small[:, 0:1], minus_half[:, 0:1], ACT.Copy).then_inc(s_all, 1)
                    act.wait_ge(s_eys[1], last * 8)
                    act.activation(small[:, 1:2], minus_half[:, 0:1], ACT.Copy).then_inc(s_all, 1)
                    for t in range(NT):
                        ya = yab[:, t % 2, 0, :]
                        act.wait_ge(s_cg[t % 2], 32 * (t // 2 + 1))
                        act.activation(ya, ya, ACT.Copy, scale=wpair[:, 0, t:t + 1]).then_inc(s_ca, 1)

                @block.vector
                def _(dve):
                    def out(j, par, least):
                        dve.wait_ge(s_ey, j + 1)
                        if least >= 2:
                            dve.wait_ge(s_eys[par], (j - par) * 8)
                        dve.tensor_copy(ys[:, par, :], PS[:, 6:8, :].rearrange("p b n -> p (b n)")).then_inc(s_eye, 1)

                    def step(j, par, least):
                        dve.wait_ge(s_esg, j + 1)
                        dve.tensor_tensor(sg[:, par, :], PS[:, 2 + par, 0:DE], sg[:, par, :], ALU.mult)\
                           .then_inc(s_et1, 1)
                        dve.wait_ge(s_et1, j + 1)
                        if least >= 2:
                            dve.wait_ge(s_etr, j - 1)
                        dve.tensor_tensor(ha[:, par, :], sg[:, par, :], PS[:, 2 + par, DE:2 * DE], ALU.mult)\
                           .then_inc(s_eh, 1)
                        if least >= 1:
                            out(j - 1, 1 - par, least - 1)
                    over_tiles(dve, step, 0)
                    out(load_last(dve), 0, 2)
                    for t in range(NT):
                        ya, yb = yab[:, t % 2, 0, :], yab[:, t % 2, 1, :]
                        dve.wait_ge(s_ca, t + 1)
                        dve.scalar_tensor_tensor(ya, yb, wpair[:, 1, t:t + 1], ya, ALU.mult, ALU.add).then_inc(s_cm, 1)
                        dve.wait_ge(s_cm, 3 * t + 1)
                        dve.tensor_tensor(ya, ya, g2b[:, 1 if t else 0, :], ALU.mult).then_inc(s_cm, 1)
                        dve.wait_ge(s_cm, 3 * t + 2)
                        dve.tensor_tensor(x[:, t, :], x[:, t, :], ya, ALU.add).then_inc(s_cm, 1)

            with nc.Block() as block:
                @block.gpsimd
                def _(pool):
                    pool.dma_reset(range(layer_sems[0].num, layer_sems[-1].num + 1))
                    for s in layer_sems:
                        pool.sem_clear(s)
            lay_ctx.close()

        with ExitStack() as fin_ctx:
            s_fl, s_fs, s_fm, s_fp, s_fx, s_fv, s_fo = (
                fin_ctx.enter_context(nc.semaphore(n)) for n in
                ("final_load", "final_sq", "final_mean", "final_rstd", "final_scaled", "final_vec", "final_stored"))
            fg = T[:, 0:D]
            yo = T[:, D:D + NT * D].rearrange("p (t n) -> p t n", t=NT)
            ss, ms, rs = small[:, 64:64 + NT], small[:, 72:72 + NT], small[:, 80:80 + NT]
            with nc.Block() as block:
                @block.sync
                def _(sp):
                    sp.dma_start(fg, final_g.partition_broadcast(P)).then_inc(s_fl, 16)
                    for t in range(NT):
                        sp.wait_ge(s_fv, t + 1)
                        dst = y_prompt[0] if t == 0 else y_sample[0, (t - 1) * P:t * P, :]
                        sp.dma_start(dst, yo[:, t, :]).then_inc(s_fo, 16)
                    sp.wait_ge(s_fo, NT * 16)

                @block.scalar
                def _(act):
                    for t in range(NT):
                        act.activation(yo[:, t, :], x[:, t, :], ACT.Square, accum_out=ss[:, t:t + 1]).then_inc(s_fs, 1)
                    act.wait_ge(s_fp, 1)
                    act.wait_ge(s_fs, NT)
                    for t in range(NT):
                        act.activation(yo[:, t, :], x[:, t, :], ACT.Copy, scale=rs[:, t:t + 1]).then_inc(s_fx, 1)

                @block.gpsimd
                def _(pool):
                    pool.wait_ge(s_fm, 1)
                    pool.tensor_tensor(rs, ms, minus_half[:, 0:NT], ALU.pow).then_inc(s_fp, 1)

                @block.vector
                def _(dve):
                    dve.wait_ge(s_fs, NT)
                    dve.tensor_scalar(ms, ss, 1.0 / D, EPS, ALU.mult, ALU.add).then_inc(s_fm, 1)
                    dve.wait_ge(s_fl, 16)
                    for t in range(NT):
                        dve.wait_ge(s_fx, t + 1)
                        dve.tensor_tensor(yo[:, t, :], yo[:, t, :], fg, ALU.mult).then_inc(s_fv, 1)


def constants():
    import numpy as np
    cst = np.zeros((P, C_END), np.float32)
    cst[:, C_IDENT:C_IDENT + P] = np.eye(P)
    p, j = np.arange(P)[:, None], np.arange(P)[None, :]
    cst[:, C_WIN:C_WIN + P] = np.where(j >= p, 0.0, -1e30)
    cst[:, C_WIN + 3 * P:C_WIN + 4 * P] = np.where(j <= p, 0.0, -1e30)
    n_freq = HD // 4
    freqs = (np.float32(10000.0) ** (-np.arange(n_freq, dtype=np.float32) / np.float32(n_freq))).astype(np.float32)
    tok = np.arange(NL * P)
    pos = np.stack([tok // 64, tok % 64], 1).astype(np.float32)
    angle = (pos[:, :, None] * freqs).astype(np.float32).reshape(NL, P, 2 * n_freq)
    pair = np.concatenate([angle, angle], 2)
    cst[:, C_COS:C_COS + 2 * P] = np.cos(pair).transpose(1, 0, 2).reshape(P, 2 * P)
    cst[:, C_SIN:C_SIN + 2 * P] = np.sin(pair).transpose(1, 0, 2).reshape(P, 2 * P)
    i4, j4 = np.arange(4)[:, None], np.arange(4)[None, :]
    cst[:, C_LT:C_LT + 16] = (j4 < i4).astype(np.float32).reshape(1, 16)
    masks = np.zeros((P, 2, len(LEVELS) + 1, P), np.float32)
    s, t = p, j
    masks[:, :, 0] = (s == t)[:, None, :]
    for lv, h in enumerate(LEVELS, start=1):
        same = (s // (2 * h)) == (t // (2 * h))
        low, high = (s // h) % 2 == 0, (t // h) % 2 == 1
        masks[:, 0, lv] = same & low & high
        masks[:, 1, lv] = same & ~low & ~high
    route = np.zeros((P, RC_END), np.float32)
    route[:, RC_BEFORE:RC_BEFORE + P] = p < j
    route[:, RC_ONES:RC_ONES + P] = 1.0
    route[:, RC_TILE:RC_TILE + NS] = np.arange(NS)
    route[:, RC_TOKEN:RC_TOKEN + NT] = p + P * np.arange(NT)
    route[:, RC_IOTA:RC_IOTA + P] = j
    return cst, masks.reshape(P, -1), route


_INS = ["x_prompt", "x_sample", "cache_glob_k", "cache_glob_v", "cache_win_k", "cache_win_v", "state_hgrn", "c",
        "c_ctx", "mod_w", "mod_b", "norm1_g", "norm2_g", "w_in", "w_out", "hgrn_lb", "hgrn_norm_g", "q_norm_g",
        "k_norm_g", "win_sink", "router_w", "router_b", "w_gate_up", "w_down", "final_g"]
_OUTS = [(1, P, D), (1, NL * P, D)] + [(1, DEPTH, P, KVH, HD)] * 4 + [(1, DEPTH, 2, AH, HD, HD)]


def kernel(**inputs):
    import numpy as np
    import concourse.bacc as bacc
    from concourse.bass_utils import run_bass_kernel_spmd

    nc = bacc.Bacc("TRN2", target_bir_lowering=False, num_devices=1)
    arrays, args = {}, []
    cst, masks, route = constants()
    for name, a in [(n, inputs[n]) for n in _INS] + [("consts", cst), ("masks", masks), ("route", route)]:
        a = np.ascontiguousarray(a)
        arrays[f"in_{name}"] = a
        args.append(nc.dram_tensor(f"in_{name}", a.shape, mybir.dt.from_np(a.dtype), kind="ExternalInput").ap())
    for i, shape in enumerate(_OUTS):
        args.append(nc.dram_tensor(f"out_{i}", shape, F32, kind="ExternalOutput").ap())
    program(nc, *args)
    r = run_bass_kernel_spmd(nc, [arrays], core_ids=[0])
    return tuple(r.results[0][f"out_{i}"] for i in range(len(_OUTS)))
```
